# Optimizing a Trainium2 kernel written in Bass

```python
import math
import jax, jax.numpy as jnp
from jax import lax
import numpy as np

D_MODEL = 2048
BATCH = 1
SEQ = 256
DEPTH = 1

GLA_HEADS = 4
GLA_DK = D_MODEL // 2
GLA_DV = D_MODEL
GLA_HK = GLA_DK // GLA_HEADS
GLA_HV = GLA_DV // GLA_HEADS
GLA_RANK = 16
GLA_TAU = 16.0
GLA_CHUNK = 64
FOX_HEADS = 16
FOX_HD = D_MODEL // FOX_HEADS
FOX_BLOCK = 128
FOX_W = FOX_HEADS * FOX_HD
D_FF = 4 * D_MODEL
N_MOD = 6
EPS = 1e-6

IN_SIZES = (GLA_DK, GLA_DK, GLA_DV, GLA_DV, GLA_RANK,
            FOX_W, FOX_W, FOX_W, FOX_HEADS,
            D_MODEL, D_MODEL)
D_IN = 2 * GLA_DK + 2 * GLA_DV + GLA_RANK + 3 * FOX_W + FOX_HEADS + 2 * D_MODEL

kernel_name = "hybrid_gla_fox_adaln_block"

def _split_points():
    return [int(v) for v in np.cumsum(np.array(IN_SIZES))[:-1]]

def rms_norm(x, g):
    xf = x.astype(jnp.float32)
    y = xf * lax.rsqrt(jnp.mean(xf * xf, axis=-1, keepdims=True) + EPS)
    return (y * g.astype(jnp.float32)).astype(x.dtype)

def to_heads(t, n):
    b, s, _ = t.shape
    return t.reshape(b, s, n, -1).transpose(0, 2, 1, 3)

def merge_heads(t):
    b, h, s, d = t.shape
    return t.transpose(0, 2, 1, 3).reshape(b, s, h * d)

def gla_chunked(q, k, v, log_a):
    B, H, S, dk = q.shape
    dv = v.shape[-1]
    n_chunks = S // GLA_CHUNK

    def chunks(t):
        return t.astype(jnp.float32).reshape(B, H, n_chunks, GLA_CHUNK, t.shape[-1]).transpose(2, 0, 1, 3, 4)

    causal = jnp.tril(jnp.ones((GLA_CHUNK, GLA_CHUNK), dtype=bool))

    def step(state, inp):
        qc, kc, vc, lac = inp
        b = jnp.cumsum(lac, axis=-2)
        b_last = b[..., -1:, :]
        q_dec = qc * jnp.exp(b)
        attn = jnp.einsum('bhtd,bhsd->bhts', q_dec, kc * jnp.exp(-b))
        attn = jnp.where(causal, attn, 0.0)
        o = jnp.einsum('bhts,bhsv->bhtv', attn, vc) + jnp.einsum('bhtd,bhdv->bhtv', q_dec, state)
        k_dec = kc * jnp.exp(b_last - b)
        state = state * jnp.swapaxes(jnp.exp(b_last), -1, -2) + jnp.einsum('bhsd,bhsv->bhdv', k_dec, vc)
        return state, o

    state0 = jnp.zeros((B, H, dk, dv), jnp.float32)
    _, o = lax.scan(step, state0, (chunks(q), chunks(k), chunks(v), chunks(log_a)))
    return o.transpose(1, 2, 0, 3, 4).reshape(B, H, S, dv).astype(v.dtype)

def forgetting_attention(q, k, v, log_f):
    S = q.shape[2]
    scale = 1.0 / math.sqrt(q.shape[-1])
    cum = jnp.cumsum(log_f, axis=-1)
    outs = []
    for i in range(S // FOX_BLOCK):
        q0, end = i * FOX_BLOCK, (i + 1) * FOX_BLOCK
        qb = q[:, :, q0:end]
        kb, vb = k[:, :, :end], v[:, :, :end]
        s = jnp.einsum('bhtd,bhsd->bhts', qb, kb).astype(jnp.float32) * scale
        s = s + cum[:, :, q0:end, None] - cum[:, :, None, :end]
        qpos = jnp.arange(q0, end)[:, None]
        kpos = jnp.arange(end)[None, :]
        s = jnp.where(kpos <= qpos, s, -jnp.inf)
        p = jax.nn.softmax(s, axis=-1).astype(v.dtype)
        outs.append(jnp.einsum('bhts,bhsd->bhtd', p, vb))
    return jnp.concatenate(outs, axis=2)

def setup_inputs(seed: int = 0) -> dict:
    key = jax.random.key(seed)
    ks = jax.random.split(key, 20)
    f32 = jnp.float32
    nrm = lambda k, shape, s: jax.random.normal(k, shape, f32) * s
    D = D_MODEL
    return {
        "x": nrm(ks[0], (BATCH, SEQ, D), 1.0),
        "c": nrm(ks[1], (BATCH, D), 1.0),
        "w_ada": nrm(ks[2], (DEPTH, D, N_MOD * D), 0.5 * D ** -0.5),
        "b_ada": nrm(ks[3], (DEPTH, N_MOD * D), 0.01),
        "g_norm1": 1.0 + nrm(ks[4], (DEPTH, D), 0.05),
        "w_in": nrm(ks[5], (DEPTH, D, D_IN), D ** -0.5),
        "w_gla_a_up": nrm(ks[6], (DEPTH, GLA_RANK, GLA_DK), GLA_RANK ** -0.5),
        "b_gla_a": 1.0 + nrm(ks[7], (DEPTH, GLA_DK), 0.5),
        "g_gla_out": 1.0 + nrm(ks[8], (DEPTH, GLA_HV), 0.05),
        "b_fox_f": 2.0 + nrm(ks[9], (DEPTH, FOX_HEADS), 1.0),
        "w_proj_gla": nrm(ks[10], (DEPTH, GLA_DV, D), GLA_DV ** -0.5),
        "w_proj_fox": nrm(ks[11], (DEPTH, FOX_W, D), FOX_W ** -0.5),
        "w_out": nrm(ks[12], (DEPTH, D, D), D ** -0.5),
        "g_norm2": 1.0 + nrm(ks[13], (DEPTH, D), 0.05),
        "w_ff1": nrm(ks[14], (DEPTH, D, D_FF), D ** -0.5),
        "w_ff2": nrm(ks[15], (DEPTH, D_FF, D), D_FF ** -0.5),
        "g_final": 1.0 + nrm(ks[16], (D,), 0.05),
    }

def reference(x, c, w_ada, b_ada, g_norm1, w_in, w_gla_a_up, b_gla_a, g_gla_out, b_fox_f,
              w_proj_gla, w_proj_fox, w_out, g_norm2, w_ff1, w_ff2, g_final):
    cond = jax.nn.silu(c)
    split_pts = _split_points()
    for l in range(DEPTH):
        mod = (cond @ w_ada[l] + b_ada[l])[:, None, :]
        shift1, scale1, gate1, shift2, scale2, gate2 = jnp.split(mod, N_MOD, axis=-1)

        h = rms_norm(x, g_norm1[l]) * (1.0 + scale1) + shift1
        proj = h @ w_in[l]
        (gq, gk, gv, gg, ga_low, fq, fk, fv, f_logit, gate_a, gate_b) = jnp.split(proj, split_pts, axis=-1)

        log_a = jax.nn.log_sigmoid((ga_low @ w_gla_a_up[l] + b_gla_a[l]).astype(jnp.float32)) / GLA_TAU
        o_a = gla_chunked(to_heads(gq * (GLA_HK ** -0.5), GLA_HEADS), to_heads(gk, GLA_HEADS),
                          to_heads(gv, GLA_HEADS), to_heads(log_a, GLA_HEADS))
        o_a = merge_heads(rms_norm(o_a, g_gla_out[l])) * jax.nn.silu(gg)

        log_f = jax.nn.log_sigmoid((f_logit + b_fox_f[l]).astype(jnp.float32)).transpose(0, 2, 1)
        o_b = merge_heads(forgetting_attention(to_heads(fq, FOX_HEADS), to_heads(fk, FOX_HEADS),
                                               to_heads(fv, FOX_HEADS), log_f))

        merged = jax.nn.sigmoid(gate_a) * (o_a @ w_proj_gla[l]) + jax.nn.sigmoid(gate_b) * (o_b @ w_proj_fox[l])
        x = x + gate1 * (merged @ w_out[l])

        h2 = rms_norm(x, g_norm2[l]) * (1.0 + scale2) + shift2
        x = x + gate2 * (jnp.square(jax.nn.relu(h2 @ w_ff1[l])) @ w_ff2[l])
    return rms_norm(x, g_final)


_drawn_inputs = setup_inputs


def setup_inputs(seed=0):
    import zlib

    import numpy as np

    out = dict(_drawn_inputs(seed))
    spreads = {}
    factors = {'b_ada': 3.465, 'g_norm1': 4.654, 'g_gla_out': 8.0, 'g_norm2': 8.0}
    for name, (base, spread) in spreads.items():
        noise = np.random.default_rng([zlib.crc32(name.encode()), seed]).standard_normal(out[name].shape)
        drawn = base * np.exp(spread * noise) if base else spread * noise
        out[name] = __import__('jax').numpy.asarray(drawn.astype(out[name].dtype))
    for name, factor in factors.items():
        out[name] = (out[name] * factor).astype(out[name].dtype)
    return out
```

```python
import concourse.bass as bass
from concourse import mybir

F32 = mybir.dt.float32
F32R = mybir.dt.float32r
ACT = mybir.ActivationFunctionType
ALU = mybir.AluOpType
AX_X = mybir.AxisListType.X

P = 128
D = 2048
S = 256
TT = S // P
KT = D // P
NB = 512
KU = 2
UG = KT // KU
LEAD = 3
RING = 4
EPS = 1e-6
BIG = 3.4e38
HK, HV = 256, 512
CH = 64
NC = S // CH
RANK = 16
TAU = 16.0
FH, FD = 16, 128
FSC = FD ** -0.5
GSC = HK ** -0.5

C_GQ, C_GK, C_GV, C_GG, C_LOW = 0, 1024, 2048, 4096, 6144
C_FQ, C_FK, C_FV, C_FL, C_GA, C_GB = 6160, 8208, 10256, 12304, 12320, 14368

FOX = dict(its=4, n=24, ada=[8, 9, 10, 11, 12, 13, 14, 16], ev=10, tr=8, bk=7)
GLA = dict(its=4, n=24, ada=[8, 9, 10, 11, 12, 13, 14, 16], ev=8, tr=4, bk=5)
MIX = dict(its=4, n=32, ada=[1, 2, 3, 4, 5, 6, 9, 11, 14, 16, 17, 18, 19, 20, 21, 22], ev=16, tr=16, bk=12)
OUT = dict(its=1, n=32, ada=[], ev=8, tr=0, bk=4)
FF = dict(its=4, n=64, ada=[], ev=24, tr=16, bk=16)
ADA0 = 8


def lay_out_phases():
    g, u, e, w, a, b = 1, ADA0 * UG + 1, 0, 0, ADA0, 0
    for ph in (FOX, GLA, MIX, OUT, FF):
        ph.update(g0=g, u0=u, e0=e, w0=w, a0=a, b0=b, nu=ph["n"] + len(ph["ada"]), na=len(ph["ada"]) // UG)
        order, pos_g, pos_a = 0, [], []
        for x in range(ph["n"] + LEAD):
            pos_g.append(order)
            order += 1
            slot = x - LEAD
            for s in ph["ada"]:
                if s == slot:
                    pos_a.append(order)
                    order += 1
        assert pos_g[ph["n"]] == ph["nu"] and order == ph["nu"] + LEAD
        ph.update(pos_g=pos_g, pos_a=pos_a)
        g += ph["its"] * ph["n"]
        u += ph["its"] * ph["nu"]
        e += ph["its"] * ph["ev"]
        w += ph["its"] * ph["tr"]
        a += ph["its"] * ph["na"]
        b += ph["its"] * ph["bk"]


lay_out_phases()


def build(nc, x, c, w_ada, b_ada, g_norm1, w_in, w_gla_a_up, b_gla_a, g_gla_out, b_fox_f,
          w_proj_gla, w_proj_fox, w_out, g_norm2, w_ff1, w_ff2, g_final, out):
    base = (nc.sbuf_base + 31) // 32 * 32
    offset = [base]

    def region(size):
        offset[0] += size
        assert offset[0] <= nc.sbuf_usable_end, (offset[0], nc.sbuf_usable_end)
        return offset[0] - size

    def at(name, shape, off, dt=F32):
        return nc.alloc_sbuf_tensor_at(name, shape, dt, offset=off)

    def new(name, shape, dt=F32):
        size = 4
        for n in shape[1:]:
            size *= n
        return at(name, shape, region((size + 31) // 32 * 32), dt)

    raw = [new(f"raw{i}", [P, KU, NB]) for i in range(RING)]
    whi = [new(f"whi{i}", [P, KU, NB], F32R) for i in range(RING)]
    wlo = [new(f"wlo{i}", [P, KU, NB], F32R) for i in range(RING)]
    hT = new("hT", [P, KT, 2, S], F32R)
    obT = new("obT", [P, KT, 2, S], F32R)
    r1 = region(KT * 2 * S * 4)
    oaT = at("oaT", [P, KT, 2, S], r1, F32R)
    x_in = at("x_in", [P, TT, D], r1)
    xT = at("xT", [P, KT, S], r1)
    ncrow = at("ncrow", [1, FH, S], r1)
    xn = at("xn", [P, TT, D], r1 + 16384)
    y_out = at("y_out", [P, TT, D], r1)
    rm = region(KT * S * 4)
    mT = at("mT", [P, KT, S], rm)
    xl = at("xl", [P, TT, D], rm)
    fq = at("fq", [P, 4, S], rm)
    fk = at("fk", [P, 4, S], rm + 4096)
    fv = at("fv", [P, TT, NB], rm + 8192)
    fs = at("fs", [P, 2, 3 * P], rm + 12288)
    gs = region(12288)
    gq = at("gq", [P, 2, S], gs)
    gk = at("gk", [P, 2, S], gs + 2048)
    gv = at("gv", [P, TT, NB], gs + 4096)
    gg = at("gg", [P, TT, NB], gs + 8192)
    la = at("la", [P, TT, 2, NB], gs)
    gt = region(15360)
    qd = at("qd", [P, 2, S], gt)
    kd = at("kd", [P, 2, S], gt + 2048)
    ep = at("ep", [P, 2, S], gt + 4096)
    ki = at("ki", [P, 2, S], gt + 6144)
    qv1 = at("qv1", [P, 2, 2, CH], gt + 8192)
    qv2 = at("qv2", [P, 2, CH], gt + 9216)
    ot = at("ot", [P, TT, NB], gt + 9728)
    am = at("am", [P, 3, P], gt + 13824)
    wup = at("wup", [RANK + 1, 2, NB], gt)
    tsm = at("tsm", [CH, S], gt + 4096)
    sm = at("sm", [CH, S], gt + 5120)
    zm = at("zm", [CH, S], gt + 6144)
    ab = at("ab", [CH, S], gt + 7168)
    gl = at("gl", [RANK + 1, S], gt + 8192)
    nct = at("nct", [FH, S], gt + 7168)
    tri = at("tri", [P, P], gt + 9216)
    tri16 = at("tri16", [P, P], gt + 9728)
    fm = at("fm", [P, 3 * P], gt + 10240)
    pT = at("pT", [P, 3 * P], gt + 11776)
    lft = at("lft", [P, TT, FH], gt + 13312)
    rb = region(8192)
    bT = at("bT", [P, 8, S], rb)
    lm = at("lm", [P, TT, 2, NB], rb)
    gz = at("gz", [P, 4, S], rb)
    mt = at("mt", [P, 2, S], rb + 4096)
    gfin = at("gfin", [P, D], rb)
    gate1 = at("gate1", [P, D], gs)
    gate2 = at("gate2", [P, D], gs + 8192)
    t5 = at("t5", [P, 2, NB], gs + 16384)
    ident = new("ident", [P, P])
    ones = new("ones", [P, P])
    mhi = new("mhi", [P, P])
    mlo = new("mlo", [P, P])
    tmp = new("tmp", [P, 2, S])
    acc = new("acc", [P, 2, NB])
    bi = new("bi", [P, NB])
    gout = new("gout", [P, HV])
    modc = new("modc", [P, 4, KT])
    gcol = new("gcol", [P, 2, KT])
    cond = new("cond", [P, KT])
    vrow = at("vrow", [2 * KT, P], gs)
    ctmp = at("ctmp", [P, KT], gs + 512)
    ctm2 = at("ctm2", [P, KT], gs + 576)
    cumc = new("cumc", [P, TT, FH])
    bf = new("bf", [CH, 1])
    neghalf = new("neghalf", [P, 2])
    nst = new("nst", [P, 6, 2])
    fst = new("fst", [P, 2, 6])
    ps = [nc.alloc_psum_tensor(f"ps{i}", [P, 512], F32) for i in range(8)]

    s_go_on = nc.alloc_semaphore("s_go_on")
    s_c = nc.alloc_semaphore("s_c")
    s_vrow = nc.alloc_semaphore("s_vrow")
    s_x = nc.alloc_semaphore("s_x")
    s_gout = nc.alloc_semaphore("s_gout")
    s_wup = nc.alloc_semaphore("s_wup")
    s_bf = nc.alloc_semaphore("s_bf")
    s_bi = nc.alloc_semaphore("s_bi")
    s_rowcum = nc.alloc_semaphore("s_rowcum")
    s_xl = nc.alloc_semaphore("s_xl")
    s_gfin = nc.alloc_semaphore("s_gfin")
    s_out = nc.alloc_semaphore("s_out")
    s_small = nc.alloc_semaphore("s_small")
    s_ident = nc.alloc_semaphore("s_ident")
    s_ones = nc.alloc_semaphore("s_ones")
    s_mask = nc.alloc_semaphore("s_mask")
    s_init = nc.alloc_semaphore("s_init")
    s_vt = nc.alloc_semaphore("s_vt")
    s_gcol = nc.alloc_semaphore("s_gcol")
    s_ce = nc.alloc_semaphore("s_ce")
    s_cd = nc.alloc_semaphore("s_cd")
    s_cond = nc.alloc_semaphore("s_cond")
    s_nss = nc.alloc_semaphore("s_nss")
    s_nms = nc.alloc_semaphore("s_nms")
    s_ny = nc.alloc_semaphore("s_ny")
    s_nr = nc.alloc_semaphore("s_nr")
    s_xna = nc.alloc_semaphore("s_xna")
    s_xnd = nc.alloc_semaphore("s_xnd")
    s_xt = nc.alloc_semaphore("s_xt")
    s_xte = nc.alloc_semaphore("s_xte")
    s_acol = nc.alloc_semaphore("s_acol")
    s_ap = nc.alloc_semaphore("s_ap")
    s_hh = nc.alloc_semaphore("s_hh")
    s_hl = nc.alloc_semaphore("s_hl")
    s_hi = nc.alloc_semaphore("s_hi")
    s_lo = nc.alloc_semaphore("s_lo")
    s_pe = nc.alloc_semaphore("s_pe")
    s_ada = nc.alloc_semaphore("s_ada")
    s_modmm = nc.alloc_semaphore("s_modmm")
    s_mod = nc.alloc_semaphore("s_mod")
    s_bank = nc.alloc_semaphore("s_bank")
    s_tmp = nc.alloc_semaphore("s_tmp")
    s_evac = nc.alloc_semaphore("s_evac")
    s_sma = nc.alloc_semaphore("s_sma")
    s_smd = nc.alloc_semaphore("s_smd")
    s_gl = nc.alloc_semaphore("s_gl")
    s_fz = nc.alloc_semaphore("s_fz")
    s_fa = nc.alloc_semaphore("s_fa")
    s_lf = nc.alloc_semaphore("s_lf")
    s_ft = nc.alloc_semaphore("s_ft")
    s_lft = nc.alloc_semaphore("s_lft")
    s_fc = nc.alloc_semaphore("s_fc")
    s_fcd = nc.alloc_semaphore("s_fcd")
    s_az = nc.alloc_semaphore("s_az")
    s_azd = nc.alloc_semaphore("s_azd")
    s_aza = nc.alloc_semaphore("s_aza")
    s_la = nc.alloc_semaphore("s_la")
    s_bt = nc.alloc_semaphore("s_bt")
    s_btd = nc.alloc_semaphore("s_btd")
    s_qk = nc.alloc_semaphore("s_qk")
    s_S = nc.alloc_semaphore("s_S")
    s_max = nc.alloc_semaphore("s_max")
    s_exp = nc.alloc_semaphore("s_exp")
    s_ri = nc.alloc_semaphore("s_ri")
    s_p = nc.alloc_semaphore("s_p")
    s_pt = nc.alloc_semaphore("s_pt")
    s_ptc = nc.alloc_semaphore("s_ptc")
    s_pv = nc.alloc_semaphore("s_pv")
    s_ob = nc.alloc_semaphore("s_ob")
    s_bh = nc.alloc_semaphore("s_bh")
    s_e = nc.alloc_semaphore("s_e")
    s_qd = nc.alloc_semaphore("s_qd")
    s_ga = nc.alloc_semaphore("s_ga")
    s_at = nc.alloc_semaphore("s_at")
    s_am = nc.alloc_semaphore("s_am")
    s_go = nc.alloc_semaphore("s_go")
    s_ss = nc.alloc_semaphore("s_ss")
    s_gms = nc.alloc_semaphore("s_gms")
    s_gy = nc.alloc_semaphore("s_gy")
    s_gnr = nc.alloc_semaphore("s_gnr")
    s_ot = nc.alloc_semaphore("s_ot")
    s_gt = nc.alloc_semaphore("s_gt")
    s_oa = nc.alloc_semaphore("s_oa")
    s_sig = nc.alloc_semaphore("s_sig")
    s_sgd = nc.alloc_semaphore("s_sgd")
    s_gz = nc.alloc_semaphore("s_gz")
    s_gs = nc.alloc_semaphore("s_gs")
    s_m = nc.alloc_semaphore("s_m")
    s_cvh = nc.alloc_semaphore("s_cvh")
    s_cvl = nc.alloc_semaphore("s_cvl")
    s_x2 = nc.alloc_semaphore("s_x2")
    s_act = nc.alloc_semaphore("s_act")
    s_acth = nc.alloc_semaphore("s_acth")
    s_actl = nc.alloc_semaphore("s_actl")
    s_yo = nc.alloc_semaphore("s_yo")
    s_raw = [nc.alloc_semaphore(f"s_raw{i}") for i in range(RING)]
    s_rawq = [nc.alloc_semaphore(f"s_rawq{i}") for i in range(RING)]

    w_ada_v = w_ada[0].rearrange("(p k) n -> p k n", k=KT)
    w_in_v = w_in[0].rearrange("(k p) n -> p k n", p=P)
    wpa_v = w_proj_gla[0].rearrange("(k p) n -> p k n", p=P)
    wpb_v = w_proj_fox[0].rearrange("(k p) n -> p k n", p=P)
    wo_v = w_out[0].rearrange("(k p) n -> p k n", p=P)
    wf1_v = w_ff1[0].rearrange("(k p) n -> p k n", p=P)
    wf2_v = w_ff2[0].rearrange("(k p) n -> p k n", p=P)
    x_v = x[0].rearrange("(t p) d -> p t d", p=P)
    out_v = out[0].rearrange("(t p) d -> p t d", p=P)

    def g_slot(ph, g):
        return (ph["g0"] + g) % RING

    def g_no(ph, it, g):
        return it * ph["n"] + (ph["g0"] + g)

    def u_slot(ph, pos):
        return (ph["u0"] + pos) % RING

    def landed(ph, it, pos):
        return it * (16 * ph["nu"] // RING) + 16 * ((ph["u0"] + pos) // RING + 1)

    def landed_q(it, g):
        places = [u_slot(GLA, GLA["pos_g"][x]) for x in range(UG, 2 * UG)]
        mine = places[g - UG]
        return it * (16 * places.count(mine)) + 16 * places[:g - UG + 1].count(mine)

    def events(ph, it, e=0):
        return it * ph["ev"] + (ph["e0"] + e)

    def turned(ph, it, w=0):
        return it * ph["tr"] + (ph["w0"] + w)

    def bank_done(eng, ph, it, g, b, j, banks):
        if j == banks - 1:
            eng.wait_ge(s_pe, g_no(ph, it, g) + 1)
        else:
            eng.wait_ge(s_bank, it * ph["bk"] + (ph["b0"] + b + j + 1))

    def ada_no(ph, it, a=0):
        return it * ph["na"] + (ph["a0"] + a)

    with nc.Block() as block:

        @block.sync
        def _(sp):
            def load(dst, src, freed, uslot, sem=None):
                if freed:
                    sp.wait_ge(*freed)
                    sp.sem_inc(s_go_on, 1)
                sp.dma_start(dst, src).then_inc(sem or s_raw[uslot], 16)

            def load_ada(ag, freed, uslot, mm, col):
                if mm == 0:
                    if isinstance(ag, int) and ag == 0:
                        pass
                    else:
                        sp.wait_ge(s_ada, ag * (2 * UG) - (2 * UG - 2))
                        sp.sem_inc(s_go_on, 1)
                    sp.dma_start(bi[0:1, :], b_ada[0:1, bass.ds(col, NB)]).then_inc(s_bi, 16)
                load(raw[uslot][:], w_ada_v[:, KU * mm:KU * mm + KU, bass.ds(col, NB)], freed, uslot)

            sp.wait_ge(s_init, 1)
            for n in range(2):
                for mm in range(UG):
                    u = UG * n + mm
                    load_ada(n, (s_ada, 2 * (u - RING + 1)) if u >= RING else None, u % RING, mm, n * NB)
            with sp.Fori(2, ADA0) as n:
                col = sp.snap(n * NB)
                for mm in range(UG):
                    load_ada(n, (s_ada, n * (2 * UG) + 2 * (mm - RING + 1)), mm % RING, mm, col)
            u = ADA0 * UG
            small = raw[u % RING][:].rearrange("p k n -> p (k n)").rearrange("p (k n) -> p k n", k=KT)
            sp.wait_ge(s_small, 1)
            sp.dma_start(small[:, :, 0:RANK], w_in_v[:, :, C_LOW:C_LOW + RANK],
                         ).then_inc(s_small, 16)
            sp.dma_start(small[:, :, 32:32 + FH], w_in_v[:, :, C_FL:C_FL + FH],
                         ).then_inc(s_raw[u % RING], 16)

            def body(ph, it, source, ada_col):
                src = {}
                for g in range(ph["n"]):
                    src[ph["pos_g"][g]] = ("g", g)
                for k, pos in enumerate(ph["pos_a"]):
                    src[pos] = ("a", k)
                for k in range(1, RING + 1):
                    src[-k] = ("g", -k)
                if ph is FOX and isinstance(it, int):
                    for k in range(2, RING + 1):
                        src[-k] = ("first", ADA0 * UG + 1 - k)
                for pos in range(ph["nu"]):
                    kind, k = src[pos - RING]
                    if kind == "g":
                        freed = (s_lo, g_no(ph, it, k) + 1)
                    elif kind == "a":
                        freed = (s_ada, ada_no(ph, it, k // UG) * (2 * UG) + 2 * (k % UG + 1))
                    else:
                        freed = (s_ada, 2 * (k + 1))
                    kind, k = src[pos]
                    us = u_slot(ph, pos)
                    if kind == "a":
                        load_ada(ada_no(ph, it, k // UG), freed, us, k % UG, ada_col[k // UG])
                    else:
                        load(*source(k, us, freed), freed, us)

            def phase(ph, make):
                if ph["its"] == 1:
                    body(ph, 0, *make(0))
                    return
                if ph is FOX:
                    body(ph, 0, *make(0))
                with sp.Fori(1 if ph is FOX else 0, ph["its"]) as it:
                    body(ph, it, *make(it))

            def snap(v):
                return v if isinstance(v, int) else sp.snap(v)

            def fox(it):
                cols = [snap(it * NB + cc) for cc in (C_FQ, C_FK, C_FV)]
                return (lambda g, us, _: (raw[us][:], w_in_v[:, KU * (g % UG):KU * (g % UG) + KU,
                                                    bass.ds(cols[g // UG], NB)]),
                        [snap(it * NB + 3 * D)])

            def gla(it):
                qc, kc = snap(it * HK + C_GQ), snap(it * HK + C_GK)
                cols = [snap(it * NB + C_GG), None, snap(it * NB + C_GV)]

                def source(g, us, freed):
                    r = raw[us]
                    ks = slice(KU * (g % UG), KU * (g % UG) + KU)
                    if g // UG == 1:
                        load(r[:, :, 0:HK], w_in_v[:, ks, bass.ds(qc, HK)], freed, us, s_rawq[us])
                        return r[:, :, HK:2 * HK], w_in_v[:, ks, bass.ds(kc, HK)]
                    return r[:], w_in_v[:, ks, bass.ds(cols[g // UG], NB)]
                return source, [snap(it * NB + 4 * D)]

            def mix(it):
                n0 = snap(it * NB)
                cols = [snap(it * NB + C_GB), n0, snap(it * NB + C_GA), n0]
                views = [w_in_v, wpb_v, w_in_v, wpa_v]
                return (lambda g, us, _: (raw[us][:], views[g // UG][:, KU * (g % UG):KU * (g % UG) + KU,
                                                            bass.ds(cols[g // UG], NB)]),
                        [snap(it * NB + 2 * D), snap(it * NB + 5 * D)])

            def wout(it):
                return (lambda g, us, _: (raw[us][:], wo_v[:, KU * (g % UG):KU * (g % UG) + KU,
                                                  NB * (g // UG):NB * (g // UG) + NB]), [])

            def ff(it):
                cols = [snap(it * D + NB * n) for n in range(4)]
                rows = [snap(it * KT + KU * n) for n in range(UG)]

                def source(g, us, freed):
                    r = raw[us]
                    if g < 4 * UG:
                        return r[:], wf1_v[:, KU * (g % UG):KU * (g % UG) + KU, bass.ds(cols[g // UG], NB)]
                    n = g // UG - 4
                    return r[:], wf2_v[:, bass.ds(rows[g % UG], KU), NB * n:NB * n + NB]
                return source, []

            phase(FOX, fox)
            phase(GLA, gla)
            phase(MIX, mix)
            phase(OUT, wout)
            phase(FF, ff)
            for t in range(TT):
                sp.wait_ge(s_yo, t + 1)
                sp.dma_start(out_v[:, t, :], y_out[:, t, :]).then_inc(s_out, 16)
            sp.wait_ge(s_out, 16 * TT)

        @block.gpsimd
        def _(pool):
            nc.gpsimd.memset(bi[:], 0.0).then_inc(s_init, 1)
            nc.gpsimd.memset(ident[:], 0.0)
            nc.gpsimd.memset(ones[:], 1.0).then_inc(s_ones, 1)
            nc.gpsimd.memset(neghalf[:], -0.5)
            nc.gpsimd.memset(mhi[:], BIG)
            nc.gpsimd.memset(mlo[:], -BIG)
            nc.gpsimd.memset(tri[:], 1.0)
            nc.gpsimd.memset(tri16[:], 1.0 / TAU)
            nc.gpsimd.memset(fm[:], 0.0)
            nc.gpsimd.memset(am[:], 0.0)
            nc.gpsimd.memset(gl[:], 1.0).then_inc(s_init, 1)
            pool.wait_ge(s_init, 2)
            nc.gpsimd.affine_select(out=ident[:], in_=ident[:], compare_op=ALU.not_equal, fill=1.0, base=0,
                                    pattern=[[-1, P]], channel_multiplier=1).then_inc(s_ident, 1)
            for t_ in (mhi, mlo, tri, tri16):
                nc.gpsimd.affine_select(out=t_[:], in_=t_[:], compare_op=ALU.is_ge, fill=0.0, base=0,
                                        pattern=[[1, P]], channel_multiplier=-1).then_inc(s_mask, 1)
            for b in (0, 2):
                nc.gpsimd.affine_select(out=fm[:, b * P:b * P + P], in_=fm[:, b * P:b * P + P],
                                        compare_op=ALU.is_ge, fill=-1e30, base=0,
                                        pattern=[[-1, P]], channel_multiplier=1).then_inc(s_mask, 1)
            pool.wait_ge(s_mask, 6)
            nc.gpsimd.memset(tri16[0:CH, CH:P], 0.0).then_inc(s_mask, 1)

            def norm_pow(r):
                pool.wait_ge(s_nms, r + 1)
                nc.gpsimd.tensor_tensor(nst[:, 2, :], nst[:, 1, :], neghalf[:], ALU.pow).then_inc(s_ny, 1)

            norm_pow(0)
            u = ADA0 * UG
            pool.wait_ge(s_ada, 2 * (u - RING + 1))
            nc.gpsimd.memset(raw[u % RING][:], 0.0).then_inc(s_small, 1)
            pool.wait_ge(s_fcd, 2)
            nc.gpsimd.dma_start(ncrow[0:1, :, :], nct[:]).then_inc(s_rowcum, 16)
            with pool.Fori(0, 4) as h:
                pool.wait_ge(s_gms, h + 1)
                nc.gpsimd.tensor_tensor(nst[:, 2, :], nst[:, 1, :], neghalf[:], ALU.pow).then_inc(s_gy, 1)
            norm_pow(1)
            norm_pow(2)

        @block.scalar
        def _(act):
            act.dma_start(cond[:], c[0].rearrange("(p k) -> p k", k=KT)).then_inc(s_c, 16)
            act.dma_start(vrow[0:KT, :], g_norm1[0].rearrange("(k n) -> k n", n=P)).then_inc(s_vrow, 16)
            act.dma_start(vrow[KT:2 * KT, :], g_norm2[0].rearrange("(k n) -> k n", n=P)).then_inc(s_vrow, 16)
            act.dma_start(x_in[:], x_v).then_inc(s_x, 16)
            act.dma_start(gout[:], g_gla_out[0].partition_broadcast(P)).then_inc(s_gout, 16)
            act.dma_start(wup[0:RANK, :, :], w_gla_a_up[0].rearrange("r (a n) -> r a n", n=NB)).then_inc(s_wup, 16)
            act.dma_start(wup[RANK:RANK + 1, :, :], b_gla_a[0:1].rearrange("r (a n) -> r a n", n=NB)).then_inc(s_wup, 16)
            act.dma_start(bf[32:32 + FH, :], b_fox_f[0].rearrange("(h a) -> h a", a=1)).then_inc(s_bf, 16)
            act.wait_ge(s_c, 16)
            nc.scalar.activation(ctmp[:], cond[:], ACT.Exp, scale=-1.0).then_inc(s_ce, 1)

            def norm_squares(r, src):
                for t in range(TT):
                    nc.scalar.activation(xn[:, t, :], src[:, t, :], ACT.Square,
                                         accum_out=nst[:, 0, t:t + 1]).then_inc(s_nss, 1)

            def norm_rows(r, src):
                act.wait_ge(s_nr, 4 * r + 4)
                nc.scalar.activation(xn[:, 1, :], src[:, 1, :], ACT.Copy,
                                     scale=nst[:, 5, 1:2]).then_inc(s_xna, 1)

            def norm_evac(r):
                act.wait_ge(s_xna, r + 1)
                for n in range(8):
                    t, b = n // 4, n % 4
                    act.wait_ge(s_xt, 8 * r + n + 1)
                    nc.scalar.activation(xT[:, 4 * b:4 * b + 4, t * P:t * P + P],
                                         ps[b][:].rearrange("p (k n) -> p k n", k=4),
                                         ACT.Copy).then_inc(s_xte, 1)

            def norm_split(r, dst):
                for k in range(KT):
                    act.wait_ge(s_ap, KT * r + k + 1)
                    nc.scalar.activation(dst[:, k, 0, :], xT[:, k, :], ACT.Copy).then_inc(s_hh, 1)

            def prep(ph, it, g):
                pos = ph["pos_g"][g]
                us, gs_ = u_slot(ph, pos), g_slot(ph, g)
                act.wait_ge(s_raw[us], landed(ph, it, pos))
                if ph is GLA and UG <= g < 2 * UG:
                    act.wait_ge(s_rawq[us], landed_q(it, g))
                act.wait_ge(s_pe, g_no(ph, it, g) - (RING - 1))
                nc.scalar.activation(whi[gs_][:], raw[us][:], ACT.Copy).then_inc(s_hi, 1)

            def turn(ph, it, g, e, b, scales=(1.0,) * 4):
                for j in range(4):
                    bank_done(act, ph, it, g, b, j, 4)
                    need = events(ph, it, e) if j == 0 else events(ph, it, e + j - 1)
                    if not (isinstance(need, int) and need <= 0):
                        act.wait_ge(s_evac, need)
                    nc.scalar.activation(tmp[:, j % 2, :], ps[j][:, S:2 * S], ACT.Copy,
                                         scale=scales[j]).then_inc(s_tmp, 1)

            def fox_exp(n, j):
                act.wait_ge(s_max, 2 * n + 2)
                for b, sl in enumerate((slice(0, P), slice(P, 3 * P))):
                    nc.scalar.activation(fs[:, j % 2, sl], fs[:, j % 2, sl], ACT.Exp,
                                         bias=fst[:, j % 2, b:b + 1],
                                         accum_out=fst[:, j % 2, 2 + b:3 + b]).then_inc(s_exp, 1)

            def fox_turned(n, j):
                act.wait_ge(s_pt, n + 1)
                if not (isinstance(n, int) and n == 0):
                    act.wait_ge(s_pv, n)
                nc.scalar.activation(pT[:], ps[5][:, 0:3 * P], ACT.Copy).then_inc(s_ptc, 1)

            def gla_exps(h):
                act.wait_ge(s_bh, 2 * h + 1)
                nc.scalar.activation(ep[:], qd[:], ACT.Exp).then_inc(s_e, 1)
                nc.scalar.activation(ki[:], qd[:], ACT.Exp, scale=-1.0).then_inc(s_e, 1)
                act.wait_ge(s_bh, 2 * h + 2)
                nc.scalar.activation(kd[:], kd[:], ACT.Exp).then_inc(s_e, 1)

            def gla_attn(h):
                act.wait_ge(s_ga, h + 1)
                if not (isinstance(h, int) and h == 0):
                    act.wait_ge(s_go, h)
                a3 = ps[4][:, 0:3 * P]
                amf = am[:].rearrange("p a n -> p (a n)")
                for p0, p1, c0, c1 in ((0, CH, 0, 3 * P), (CH, P, CH, 2 * P), (CH, P, 2 * P + CH, 3 * P)):
                    nc.scalar.activation(amf[p0:p1, c0:c1], a3[p0:p1, c0:c1], ACT.Copy).then_inc(s_at, 1)

            def gla_squares(h):
                act.wait_ge(s_go, h + 1)
                if not (isinstance(h, int) and h == 0):
                    act.wait_ge(s_gt, 2 * h)
                for t in range(TT):
                    nc.scalar.activation(ot[:, t, :], ps[5 + t][:], ACT.Square,
                                         accum_out=nst[:, 0, t:t + 1]).then_inc(s_ss, 1)

            def gla_gate(it):
                act.wait_ge(s_evac, events(GLA, it, 2))
                nc.scalar.activation(ot[:], gg[:], ACT.Exp, scale=-1.0).then_inc(s_sig, 1)

            def gate_exp(it, e):
                act.wait_ge(s_evac, events(MIX, it, e))
                nc.scalar.activation(gz[:], gz[:], ACT.Exp, scale=-1.0).then_inc(s_gz, 1)

            def run(ph, it, steps, last=None):
                for g in range(ph["n"]):
                    if g + LEAD < (last or ph["n"] + LEAD):
                        prep(ph, it, g + LEAD)
                    for step in steps.get(g, ()):
                        step()

            act.wait_ge(s_x, 16)
            norm_squares(0, x_in)
            norm_rows(0, x_in)
            norm_evac(0)
            u = ADA0 * UG
            act.wait_ge(s_raw[u % RING], 16 * (u // RING + 1))
            act.wait_ge(s_small, 17)
            nc.scalar.activation(whi[0][:], raw[u % RING][:], ACT.Copy).then_inc(s_hi, 1)
            norm_split(0, hT)
            for g in range(LEAD):
                act.wait_ge(s_raw[u_slot(FOX, g)], landed(FOX, 0, g))
                nc.scalar.activation(whi[g_slot(FOX, g)][:], raw[u_slot(FOX, g)][:], ACT.Copy).then_inc(s_hi, 1)

            def small_turn():
                act.wait_ge(s_pe, 1)
                nc.scalar.activation(tsm[:], ps[4][0:CH, S:2 * S], ACT.Copy).then_inc(s_sma, 1)

            def small_log():
                f = slice(32, 32 + FH)
                act.wait_ge(s_fz, 1)
                nc.scalar.activation(ab[f, :], sm[f, :], ACT.Abs).then_inc(s_fa, 1)
                act.wait_ge(s_fa, 1)
                nc.scalar.activation(ab[f, :], ab[f, :], ACT.Exp, scale=-1.0).then_inc(s_fa, 1)

            def decay_abs():
                for n in range(4):
                    act.wait_ge(s_az, n + 1)
                    nc.scalar.activation(la[:, n // 2, n % 2, :], ps[4 + n][:], ACT.Abs).then_inc(s_aza, 1)
                act.wait_ge(s_aza, 4)
                nc.scalar.activation(la[:], la[:], ACT.Exp, scale=-1.0).then_inc(s_aza, 1)

            def logs():
                f = slice(32, 32 + FH)
                act.wait_ge(s_fa, 2)
                nc.scalar.activation(ab[f, :], ab[f, :], ACT.Ln, bias=1.0).then_inc(s_fa, 1)
                act.wait_ge(s_aza, 5)
                nc.scalar.activation(la[:], la[:], ACT.Ln, bias=1.0).then_inc(s_aza, 1)

            def decay_evac():
                for b in range(4):
                    act.wait_ge(s_bt, b + 1)
                    nc.scalar.activation(bT[:, 2 * b:2 * b + 2, :],
                                         ps[4 + b][:].rearrange("p (a n) -> p a n", a=2),
                                         ACT.Copy).then_inc(s_btd, 1)

            def fox_steps(it):
                st = {}
                for j in range(4):
                    n = it * 4 + j
                    st.setdefault(2 * j, []).append(lambda n=n, j=j: fox_exp(n, j))
                    st.setdefault(2 * j + 2, []).append(lambda n=n, j=j: fox_turned(n, j))
                return st

            def gla_steps(h):
                return {0: [lambda: gla_exps(h)], 3: [lambda: gla_attn(h)], 5: [lambda: gla_squares(h)]}

            def merge(*ds):
                out_ = {}
                for d_ in ds:
                    for k_, v_ in d_.items():
                        out_.setdefault(k_, []).extend(v_)
                return out_

            def fox_gemm(it):
                return {7: [lambda: turn(FOX, it, 7, 0, 0, (FSC,) * 4)], 15: [lambda: turn(FOX, it, 15, 4, 3)]}

            def gla_gemm(it):
                return {15: [lambda: turn(GLA, it, 15, 2, 1, (GSC, GSC, 1.0, 1.0)), lambda: gla_gate(it)]}

            def mix_gemm(it):
                return {7: [lambda: turn(MIX, it, 7, 0, 0), lambda: gate_exp(it, 4)],
                        15: [lambda: turn(MIX, it, 15, 4, 3)],
                        23: [lambda: turn(MIX, it, 23, 8, 6), lambda: gate_exp(it, 12)],
                        31: [lambda: turn(MIX, it, 31, 12, 9)]}

            run(FOX, 0, merge(fox_gemm(0), {0: [small_turn], 1: [small_log], 2: [decay_abs], 3: [logs],
                                            6: [decay_evac]}))
            with act.Fori(1, 4) as it:
                run(FOX, it, merge(fox_steps(it - 1), fox_gemm(it)))
            run(GLA, 0, merge(fox_steps(3), gla_gemm(0)))
            with act.Fori(1, 4) as it:
                run(GLA, it, merge(gla_steps(it - 1), gla_gemm(it)))
            run(MIX, 0, merge(gla_steps(3), mix_gemm(0)))
            with act.Fori(1, 4) as it:
                run(MIX, it, mix_gemm(it))
            act.wait_ge(s_pe, g_no(MIX, 4, 0))
            for b in range(4):
                act.wait_ge(s_m, 12 * (b + 1))
                nc.scalar.activation(hT[:, 4 * b:4 * b + 4, 0, :], mT[:, 4 * b:4 * b + 4, :],
                                     ACT.Copy).then_inc(s_cvh, 1)
            act.wait_ge(s_cvl, 4)
            act.dma_start(xl[:], x_v).then_inc(s_xl, 16)
            act.dma_start(gfin[:], g_final.partition_broadcast(P)).then_inc(s_gfin, 16)
            run(OUT, 0, {})
            act.wait_ge(s_x2, 8)
            norm_squares(1, xl)
            norm_rows(1, xl)
            norm_evac(1)
            norm_split(1, obT)

            def ff_up(it, n):
                turn(FF, it, UG * n + UG - 1, 4 * n, 3 * n)
                for j in range(4):
                    a_no = it * 16 + (4 * n + j)
                    act.wait_ge(s_act, a_no + 1)
                    nc.scalar.activation(oaT[:, 4 * n + j, 0, :], t5[:, j % 2, S:2 * S], ACT.Copy).then_inc(s_acth, 1)

            def ff_steps(it):
                return {UG * n + UG - 1: [lambda n=n: ff_up(it, n)] for n in range(4)}

            with act.Fori(0, 3) as it:
                run(FF, it, ff_steps(it))
            run(FF, 3, ff_steps(3), last=FF["n"])

            act.wait_ge(s_x2, 8 + 32)
            norm_squares(2, xl)

        @block.vector
        def _(dve):
            V = nc.vector

            dve.wait_ge(s_ce, 1)
            V.tensor_scalar(ctm2[:], ctmp[:], 1.0, None, ALU.add).then_inc(s_cd, 1)
            dve.wait_ge(s_cd, 1)
            V.reciprocal(ctmp[:], ctm2[:]).then_inc(s_cd, 1)
            dve.wait_ge(s_cd, 2)
            V.tensor_tensor(cond[:], cond[:], ctmp[:], ALU.mult).then_inc(s_cond, 1)
            dve.wait_ge(s_vt, 1)
            V.tensor_copy(gcol[:], ps[7][:, 0:2 * KT].rearrange("p (a k) -> p a k", a=2)).then_inc(s_gcol, 1)
            dve.wait_ge(s_cond, 1)

            def ada(ag, mm, us, count):
                dve.wait_ge(s_raw[us], count)
                if mm == 0:
                    dve.wait_ge(s_bi, ag * 16 + 16)
                    if not (isinstance(ag, int) and ag == 0):
                        dve.wait_ge(s_modmm, ag)
                else:
                    dve.wait_ge(s_ada, ag * (2 * UG) + 2 * mm)
                for h in range(2):
                    k = 2 * mm + h
                    if k == 1:
                        i = V.tensor_scalar(acc[:, h, :], raw[us][:, h, :], cond[:, k:k + 1], None, ALU.mult)
                    else:
                        i = V.scalar_tensor_tensor(acc[:, h, :], raw[us][:, h, :], cond[:, k:k + 1],
                                                   bi[:] if k == 0 else acc[:, h, :], ALU.mult, ALU.add)
                    i.then_inc(s_ada, 1)

            def mod_cols(ag, col):
                dve.wait_ge(s_modmm, ag + 1)
                flat = modc[:].rearrange("p a k -> p (a k)")
                V.tensor_scalar(flat[:, bass.ds(col, 4)], ps[7][:, 0:4], 1.0, None, ALU.mult).then_inc(s_mod, 1)

            def mod_row(ag, dst, col):
                dve.wait_ge(s_modmm, ag + 1)
                V.tensor_scalar(dst[:, bass.ds(col, NB)], ps[7][:], 1.0, None, ALU.mult).then_inc(s_mod, 1)

            def norm_mean(count, s_in, out_sem, n):
                dve.wait_ge(s_in, count)
                V.tensor_scalar(nst[:, 1, :], nst[:, 0, :], 1.0 / n, EPS, ALU.mult, ALU.add).then_inc(out_sem, 1)

            def newton(s_seed, count, s_own, before):
                y, t1, t2, r_ = (nst[:, n, :] for n in (2, 3, 4, 5))
                dve.wait_ge(s_seed, count)
                V.tensor_tensor(t1, y, y, ALU.mult).then_inc(s_own, 1)
                dve.wait_ge(s_own, before + 1)
                V.tensor_tensor(t2, t1, nst[:, 1, :], ALU.mult).then_inc(s_own, 1)
                dve.wait_ge(s_own, before + 2)
                V.tensor_scalar(t1, t2, -0.5, 1.5, ALU.mult, ALU.add).then_inc(s_own, 1)
                dve.wait_ge(s_own, before + 3)
                V.tensor_tensor(r_, y, t1, ALU.mult).then_inc(s_own, 1)
                dve.wait_ge(s_own, before + 4)

            def norm_rows(r, src):
                newton(s_ny, r + 1, s_nr, 4 * r)
                V.tensor_scalar(xn[:, 0, :], src[:, 0, :], nst[:, 5, 0:1], None, ALU.mult).then_inc(s_xnd, 1)

            def norm_split(r, dst):
                V.scalar_tensor_tensor(gcol[:, r, :], modc[:, 2 * r + 1, :], 1.0, gcol[:, r, :],
                                       ALU.add, ALU.mult).then_inc(s_acol, 1)
                dve.wait_ge(s_acol, r + 1)
                dve.wait_ge(s_xte, 8 * r + 8)
                for k in range(KT + 1):
                    if k < KT:
                        V.tensor_scalar(xT[:, k, :], xT[:, k, :], gcol[:, r, k:k + 1],
                                        modc[:, 2 * r, k:k + 1], ALU.mult, ALU.add).then_inc(s_ap, 1)
                    if k > 0:
                        dve.wait_ge(s_hh, KT * r + k)
                        V.tensor_tensor(dst[:, k - 1, 1, :], xT[:, k - 1, :],
                                        dst[:, k - 1, 0, :].bitcast(F32), ALU.subtract).then_inc(s_hl, 1)

            def lo(count, us, gs_):
                dve.wait_ge(s_hi, count)
                V.tensor_tensor(wlo[gs_][:], raw[us][:], whi[gs_][:].bitcast(F32),
                                ALU.subtract).then_inc(s_lo, 1)

            def prep(ph, it, g):
                lo(g_no(ph, it, g) + 1, u_slot(ph, ph["pos_g"][g]), g_slot(ph, g))

            for n in range(2):
                for mm in range(UG):
                    u = UG * n + mm
                    ada(n, mm, u % RING, 16 * (u // RING + 1))
                mod_cols(n, 4 * n)
                if n == 0:
                    norm_mean(2, s_nss, s_nms, D)
                else:
                    norm_rows(0, x_in)
            with dve.Fori(2, ADA0) as n:
                for mm in range(UG):
                    ada(n, mm, mm % RING, n * (16 * UG // RING) + 16 * (mm // RING + 1))
                mod_cols(n, n * 4)
            lo(1, ADA0 * UG % RING, 0)
            dve.wait_ge(s_mod, ADA0)
            norm_split(0, hT)
            for g in range(LEAD):
                lo(g + 2, u_slot(FOX, g), g_slot(FOX, g))

            def run(ph, it, steps, last=None):
                ada_at = {s_: k for k, s_ in enumerate(ph["ada"])}
                for g in range(ph["n"]):
                    if g + LEAD < (last or ph["n"] + LEAD):
                        prep(ph, it, g + LEAD)
                    for step in steps.get(g, ()):
                        step()
                    if g in ada_at:
                        k = ada_at[g]
                        pos = ph["pos_a"][k]
                        ada(ada_no(ph, it, k // UG), k % UG, u_slot(ph, pos), landed(ph, it, pos))

            def join(ph, it, e, w, dst, scales=(1.0,) * 4):
                for j in range(4):
                    dve.wait_ge(s_tmp, turned(ph, it, w + j) + 1)
                    if scales[j] == 1.0:
                        i = V.tensor_tensor(dst(j), ps[j][:, 0:S], tmp[:, j % 2, :], ALU.add)
                    else:
                        i = V.scalar_tensor_tensor(dst(j), ps[j][:, 0:S], scales[j], tmp[:, j % 2, :],
                                                   ALU.mult, ALU.add)
                    i.then_inc(s_evac, 1)

            def take(ph, it, g, b, banks, dst):
                for t in range(TT):
                    bank_done(dve, ph, it, g, b, t, TT)
                    V.tensor_copy(dst[:, t, :], ps[banks + t][:]).then_inc(s_evac, 1)

            f = slice(32, 32 + FH)

            def small_join():
                dve.wait_ge(s_sma, 1)
                V.tensor_tensor(sm[:], ps[4][0:CH, 0:S], tsm[:], ALU.add).then_inc(s_smd, 1)
                dve.wait_ge(s_smd, 1)
                dve.wait_ge(s_init, 2)
                V.tensor_copy(gl[0:RANK, :], sm[0:RANK, :]).then_inc(s_gl, 1)
                dve.wait_ge(s_bf, 16)
                V.tensor_scalar(sm[f, :], sm[f, :], bf[f, 0:1], None, ALU.add).then_inc(s_fz, 1)
                dve.wait_ge(s_fz, 1)
                V.tensor_scalar(zm[f, :], sm[f, :], 0.0, None, ALU.min).then_inc(s_fz, 1)

            def decay_min():
                for n in range(4):
                    dve.wait_ge(s_aza, n + 1)
                    V.tensor_scalar(lm[:, n // 2, n % 2, :], ps[4 + n][:], 0.0, None, ALU.min).then_inc(s_azd, 1)

            def log_sigmoids():
                dve.wait_ge(s_fa, 3)
                dve.wait_ge(s_fz, 2)
                V.tensor_tensor(zm[f, :], zm[f, :], ab[f, :], ALU.subtract).then_inc(s_lf, 1)
                dve.wait_ge(s_aza, 6)
                dve.wait_ge(s_azd, 4)
                V.tensor_tensor(la[:], lm[:], la[:], ALU.subtract).then_inc(s_la, 1)

            def forget_cols():
                dve.wait_ge(s_ft, 1)
                V.tensor_copy(lft[:], ps[7][:, 0:TT * FH].rearrange("p (t h) -> p t h", t=TT)).then_inc(s_lft, 1)

            def forget_cums():
                dve.wait_ge(s_fc, 1)
                V.tensor_copy(cumc[:], ps[7][:, 32:32 + TT * FH].rearrange("p (t h) -> p t h", t=TT)
                              ).then_inc(s_fcd, 1)
                V.tensor_scalar(nct[:], ps[6][0:FH, 0:S], -1.0, None, ALU.mult).then_inc(s_fcd, 1)

            halves = (slice(0, P), slice(P, 3 * P))

            def fox_scores(n, j):
                dve.wait_ge(s_qk, n + 1)
                for b, sl in enumerate(halves):
                    V.scalar_tensor_tensor(fs[:, j % 2, sl], ps[4][:, sl], cumc[:, b, bass.ds(n, 1)],
                                           fm[:, sl], ALU.add, ALU.add).then_inc(s_S, 1)
                for b, sl in enumerate(halves):
                    dve.wait_ge(s_S, n * 2 + (b + 1))
                    V.tensor_reduce(fst[:, j % 2, b:b + 1], fs[:, j % 2, sl], AX_X, ALU.max,
                                    negate=True).then_inc(s_max, 1)

            def fox_norm(n, j):
                dve.wait_ge(s_exp, n * 2 + 2)
                V.reciprocal(fst[:, j % 2, 4:6], fst[:, j % 2, 2:4]).then_inc(s_ri, 1)
                dve.wait_ge(s_ri, n + 1)
                for b, sl in enumerate(halves):
                    V.tensor_scalar(fs[:, j % 2, sl], fs[:, j % 2, sl], fst[:, j % 2, 4 + b:5 + b], None,
                                    ALU.mult).then_inc(s_p, 1)

            def fox_out(n, j):
                dve.wait_ge(s_pv, n + 1)
                o = ps[6][:, 0:S]
                V.tensor_scalar(obT[:, bass.ds(n, 1), 0, :], o, 1.0, None, ALU.mult).then_inc(s_ob, 1)
                dve.wait_ge(s_ob, n * 2 + 1)
                V.tensor_tensor(obT[:, bass.ds(n, 1), 1, :], o,
                                obT[:, bass.ds(n, 1), 0, :].bitcast(F32), ALU.subtract).then_inc(s_ob, 1)

            def fox_steps(it):
                st = {}
                for j in range(4):
                    n = it * 4 + j
                    st.setdefault(2 * j, []).append(lambda n=n, j=j: fox_scores(n, j))
                    st.setdefault(2 * j + 1, []).insert(0, lambda n=n, j=j: fox_norm(n, j))
                    st.setdefault(2 * j + 3, []).append(lambda n=n, j=j: fox_out(n, j))
                return st

            def gla_decays(h):
                bh = bT[:, bass.ds(h * 2, 2), :]
                V.tensor_scalar(qd[:], bh, 1.0, None, ALU.mult).then_inc(s_bh, 1)
                dve.wait_ge(s_bh, h * 2 + 1)
                q4 = qd[:].rearrange("p a (c t) -> p (a c) t", t=CH)
                V.tensor_tensor(kd[:].rearrange("p a (c t) -> p (a c) t", t=CH),
                                q4[:, :, CH - 1:CH].broadcast_to([P, 2 * NC, CH]), q4,
                                ALU.subtract).then_inc(s_bh, 1)

            def gla_decayed(h):
                dve.wait_ge(s_e, h * 3 + 3)
                V.tensor_tensor(qd[:], gq[:], ep[:], ALU.mult).then_inc(s_qd, 1)
                V.tensor_tensor(ki[:], gk[:], ki[:], ALU.mult).then_inc(s_qd, 1)
                V.tensor_tensor(kd[:], gk[:], kd[:], ALU.mult).then_inc(s_qd, 1)
                dve.wait_ge(s_qd, h * 5 + 1)
                last = ep[:].rearrange("p a (c t) -> p a c t", t=CH)[:, :, :, CH - 1:CH]
                for a in range(2):
                    i = V.tensor_tensor(qv1[:, a, :, :], qd[:, a, 2 * CH:4 * CH].rearrange("p (c t) -> p c t", t=CH),
                                        last[:, a, 1:3, :].broadcast_to([P, 2, CH]), ALU.mult)
                i.then_inc(s_qd, 1)
                dve.wait_ge(s_qd, h * 5 + 4)
                V.tensor_tensor(qv2[:], qv1[:, :, 1, :], last[:, :, 1, :].broadcast_to([P, 2, CH]),
                                ALU.mult).then_inc(s_qd, 1)

            def gla_mask(h):
                dve.wait_ge(s_at, h * 3 + 3)
                diag = am[:, 0:3:2, :]
                for n, (mask, op) in enumerate(((mhi, ALU.min), (mlo, ALU.max))):
                    V.tensor_tensor(diag, diag, mask[:].unsqueeze(1).broadcast_to([P, 2, P]), op).then_inc(s_am, 1)
                    dve.wait_ge(s_am, h * 2 + (n + 1))

            def gla_out(h):
                newton(s_gy, h + 1, s_gnr, h * 4)
                dve.wait_ge(s_gout, 16)
                for t in range(TT):
                    V.scalar_tensor_tensor(ot[:, t, :], ps[5 + t][:], nst[:, 5, t:t + 1], gout[:],
                                           ALU.mult, ALU.mult).then_inc(s_ot, 1)
                for t in range(TT):
                    dve.wait_ge(s_ot, h * 4 + (t + 1))
                    V.tensor_tensor(ot[:, t, :], ot[:, t, :], gg[:, t, :], ALU.mult).then_inc(s_ot, 1)
                dve.wait_ge(s_ot, h * 4 + 4)

            def gla_split(h, t):
                dve.wait_ge(s_gt, h * 2 + (t + 1))
                o = ps[4 + t][:].rearrange("p (k n) -> p k n", k=4)
                hi = oaT[:, bass.ds(h * 4, 4), 0, t * P:t * P + P]
                V.tensor_scalar(hi, o, 1.0, None, ALU.mult).then_inc(s_oa, 1)
                dve.wait_ge(s_oa, h * 4 + (2 * t + 1))
                V.tensor_tensor(oaT[:, bass.ds(h * 4, 4), 1, t * P:t * P + P], o, hi.bitcast(F32),
                                ALU.subtract).then_inc(s_oa, 1)

            def gla_steps(h):
                return {0: [lambda: gla_decays(h)], 1: [lambda: gla_decayed(h)], 4: [lambda: gla_mask(h)],
                        6: [lambda: norm_mean(h * 2 + 2, s_ss, s_gms, HV)], 7: [lambda: gla_out(h)],
                        9: [lambda: gla_split(h, 0)], 10: [lambda: gla_split(h, 1)]}

            def gla_silu(it):
                dve.wait_ge(s_sig, it + 1)
                V.tensor_scalar(ot[:], ot[:], 1.0, None, ALU.add).then_inc(s_sgd, 1)
                dve.wait_ge(s_sgd, it * 3 + 1)
                V.reciprocal(ot[:], ot[:]).then_inc(s_sgd, 1)
                dve.wait_ge(s_sgd, it * 3 + 2)
                V.tensor_tensor(gg[:], gg[:], ot[:], ALU.mult).then_inc(s_sgd, 1)

            def merge(*ds):
                out_ = {}
                for d_ in ds:
                    for k_, v_ in d_.items():
                        out_.setdefault(k_, []).extend(v_)
                return out_

            def fox_gemm(it):
                return {7: [lambda: join(FOX, it, 0, 0, lambda j: fq[:, j, :], (FSC,) * 4)],
                        15: [lambda: join(FOX, it, 4, 4, lambda j: fk[:, j, :])],
                        22: [lambda: mod_cols(ada_no(FOX, it), it * 4 + 2 * KT)],
                        23: [lambda: take(FOX, it, 23, 6, 2, fv)]}

            def gla_gemm(it):
                return {7: [lambda: take(GLA, it, 7, 0, 2, gg)],
                        15: [lambda: join(GLA, it, 2, 0, lambda j: (gq, gk)[j // 2][:, j % 2, :],
                                          (GSC, GSC, 1.0, 1.0))],
                        16: [lambda: gla_silu(it)],
                        22: [lambda: mod_cols(ada_no(GLA, it), it * 4 + 3 * KT)],
                        23: [lambda: take(GLA, it, 23, 4, 0, gv)]}

            def sigmoid(x_):
                dve.wait_ge(s_gz, x_ + 1)
                V.tensor_scalar(gz[:], gz[:], 1.0, None, ALU.add).then_inc(s_gs, 1)
                dve.wait_ge(s_gs, x_ * 2 + 1)
                V.reciprocal(gz[:], gz[:]).then_inc(s_gs, 1)

            def gated(it, e, x_, add):
                done = (lambda j: it * 12 + (4 + 2 * j if add else j))
                for j in range(4):
                    dve.wait_ge(s_tmp, turned(MIX, it, e + j) + 1)
                    V.tensor_tensor(mt[:, j % 2, :], ps[j][:, 0:S], tmp[:, j % 2, :], ALU.add).then_inc(s_evac, 1)
                    dve.wait_ge(s_evac, events(MIX, it, e + j) + 1)
                    dve.wait_ge(s_gs, x_ * 2 + 2)
                    row = mT[:, bass.ds(it * 4 + j, 1), :]
                    if not add:
                        V.tensor_tensor(row, mt[:, j % 2, :], gz[:, j, :], ALU.mult).then_inc(s_m, 1)
                    else:
                        V.tensor_tensor(mt[:, j % 2, :], mt[:, j % 2, :], gz[:, j, :], ALU.mult).then_inc(s_m, 1)
                        dve.wait_ge(s_m, done(j) + 1)
                        V.tensor_tensor(row, row, mt[:, j % 2, :], ALU.add).then_inc(s_m, 1)

            def mix_gemm(it):
                return {7: [lambda: join(MIX, it, 0, 0, lambda j: gz[:, j, :])],
                        8: [lambda: sigmoid(it * 2)],
                        13: [lambda: mod_row(ada_no(MIX, it), gate1, it * NB)],
                        15: [lambda: gated(it, 4, it * 2, False)],
                        23: [lambda: join(MIX, it, 8, 8, lambda j: gz[:, j, :])],
                        24: [lambda: sigmoid(it * 2 + 1)],
                        27: [lambda: mod_row(ada_no(MIX, it, 1), gate2, it * NB)],
                        31: [lambda: gated(it, 12, it * 2 + 1, True)]}

            run(FOX, 0, merge(fox_gemm(0), {0: [small_join], 2: [decay_min], 3: [log_sigmoids],
                                            4: [forget_cols], 5: [forget_cums]}))
            with dve.Fori(1, 4) as it:
                run(FOX, it, merge(fox_steps(it - 1), fox_gemm(it)))
            run(GLA, 0, merge(fox_steps(3), gla_gemm(0)))
            with dve.Fori(1, 4) as it:
                run(GLA, it, merge(gla_steps(it - 1), gla_gemm(it)))
            run(MIX, 0, merge(gla_steps(3), mix_gemm(0)))
            with dve.Fori(1, 4) as it:
                run(MIX, it, mix_gemm(it))
            for b in range(4):
                dve.wait_ge(s_cvh, b + 1)
                V.tensor_tensor(hT[:, 4 * b:4 * b + 4, 1, :], mT[:, 4 * b:4 * b + 4, :],
                                hT[:, 4 * b:4 * b + 4, 0, :].bitcast(F32), ALU.subtract).then_inc(s_cvl, 1)

            def residual(ph, it, g, e, b, n, gate, land):
                cols = slice(NB * n, NB * n + NB)
                for t in range(TT):
                    bank_done(dve, ph, it, g, b, t, TT)
                    V.tensor_tensor(t5[:, t, :], ps[2 * (n % 2) + t][:], gate[:, cols], ALU.mult).then_inc(s_evac, 1)
                if land:
                    dve.wait_ge(s_xl, 16)
                for t in range(TT):
                    dve.wait_ge(s_evac, events(ph, it, e + t) + 1)
                    V.tensor_tensor(xl[:, t, cols], xl[:, t, cols], t5[:, t, :], ALU.add).then_inc(s_x2, 1)

            run(OUT, 0, {UG * n + UG - 1: [lambda n=n: residual(OUT, 0, UG * n + UG - 1, 2 * n, n, n, gate1, n == 0)]
                         for n in range(4)})
            norm_mean(4, s_nss, s_nms, D)
            norm_rows(1, xl)
            norm_split(1, obT)

            def ff_up(it, n):
                def lo_of(j):
                    a_no = it * 16 + (4 * n + j)
                    dve.wait_ge(s_acth, a_no + 1)
                    V.tensor_tensor(oaT[:, 4 * n + j, 1, :], t5[:, j % 2, S:2 * S],
                                    oaT[:, 4 * n + j, 0, :].bitcast(F32), ALU.subtract).then_inc(s_actl, 1)

                for j in range(4):
                    dve.wait_ge(s_tmp, turned(FF, it, 4 * n + j) + 1)
                    V.tensor_tensor(t5[:, j % 2, 0:S], ps[j][:, 0:S], tmp[:, j % 2, :], ALU.add
                                    ).then_inc(s_evac, 1)
                    dve.wait_ge(s_evac, events(FF, it, 4 * n + j) + 1)
                    V.scalar_tensor_tensor(t5[:, j % 2, S:2 * S], t5[:, j % 2, 0:S], 0.0, t5[:, j % 2, 0:S],
                                           ALU.max, ALU.mult).then_inc(s_act, 1)
                    if j > 0:
                        lo_of(j - 1)
                lo_of(3)

            def ff_steps(it):
                st = {UG * n + UG - 1: [lambda n=n: ff_up(it, n)] for n in range(4)}
                for n in range(4):
                    st[UG * (4 + n) + UG - 1] = [lambda n=n: residual(FF, it, UG * (4 + n) + UG - 1, 16 + 2 * n, 12 + n, n, gate2, False)]
                return st

            with dve.Fori(0, 3) as it:
                run(FF, it, ff_steps(it))
            run(FF, 3, ff_steps(3), last=FF["n"])
            norm_mean(6, s_nss, s_nms, D)
            newton(s_ny, 3, s_nr, 8)
            dve.wait_ge(s_gfin, 16)
            for t in range(TT):
                V.scalar_tensor_tensor(y_out[:, t, :], xl[:, t, :], nst[:, 5, t:t + 1], gfin[:],
                                       ALU.mult, ALU.mult).then_inc(s_yo, 1)

        @block.tensor
        def _(pe):
            T = nc.tensor

            def mod_cols(ag):
                pe.wait_ge(s_ada, ag * (2 * UG) + 2 * UG)
                if isinstance(ag, int) and ag == 0:
                    pe.wait_ge(s_gcol, 1)
                else:
                    pe.wait_ge(s_mod, ag)
                for j in range(4):
                    for h in range(2):
                        i = T.matmul(ps[7][:, j:j + 1], acc[:, h, j * P:j * P + P], ones[:, 0:1],
                                     start=(h == 0), stop=(h == 1))
                i.then_inc(s_modmm, 1)

            def mod_row(ag):
                pe.wait_ge(s_ada, ag * (2 * UG) + 2 * UG)
                pe.wait_ge(s_mod, ag)
                for h in range(2):
                    i = T.matmul(ps[7][:], ones[:], acc[:, h, :], start=(h == 0), stop=(h == 1))
                i.then_inc(s_modmm, 1)

            def norm_turn(r):
                for n in range(8):
                    t, b = n // 4, n % 4
                    pe.wait_ge(s_xna if t else s_xnd, r + 1)
                    if n >= 4:
                        pe.wait_ge(s_xte, 8 * r + n - 3)
                    for k in range(4):
                        i = T.transpose(ps[b][:, k * P:k * P + P],
                                        xn[:, t, (4 * b + k) * P:(4 * b + k + 1) * P], ident[:])
                    i.then_inc(s_xt, 1)

            def banks_free(ph, it, e, deltas):
                def wait(j):
                    need = events(ph, it, e) + deltas[j]
                    if not (isinstance(need, int) and need <= 0):
                        pe.wait_ge(s_evac, need)
                return wait

            def turned_unit(ph, it, g, e, src, ready, deltas=(-3, -2, -1, 0)):
                g_ = g % UG
                sl = g_slot(ph, g)
                pe.wait_ge(s_lo, g_no(ph, it, g) + 1)
                free = banks_free(ph, it, e, deltas)
                first, final = g_ == 0, g_ == UG - 1
                order = [(j, k) for j in range(4) for k in range(KU)]
                if not first and not final:
                    order = [(j, k) for k in range(KU) for j in range(4)]
                for j, k in order:
                    kt = KU * g_ + k
                    if first and k == 0:
                        free(j)
                    if ready:
                        ready(kt)
                    w = slice(j * P, j * P + P)
                    T.matmul(ps[j][:], whi[sl][:, k, w], src[:, kt, :, :], start=(kt == 0), stop=False,
                             skip_group_check=True)
                    i = T.matmul(ps[j][:, 0:S], wlo[sl][:, k, w], src[:, kt, 0, :], start=False,
                                 stop=(kt == KT - 1), skip_group_check=True)
                    if final and k == KU - 1 and (j, k) != order[-1]:
                        i.then_inc(s_bank, 1)
                i.then_inc(s_pe, 1)

            def token_unit(ph, it, g, e, src, bank, ready, deltas=(-3, -2)):
                g_ = g % UG
                sl = g_slot(ph, g)
                pe.wait_ge(s_lo, g_no(ph, it, g) + 1)
                free = banks_free(ph, it, e, deltas)
                first, final = g_ == 0, g_ == UG - 1
                order = [(t, k) for t in range(TT) for k in range(KU)]
                for t, k in order:
                    kt = KU * g_ + k
                    if first and k == 0:
                        free(t)
                    if ready:
                        ready(kt)
                    tok = slice(t * P, t * P + P)
                    for n, (hl, w) in enumerate(((0, whi), (0, wlo), (1, whi))):
                        i = T.matmul(ps[bank + t][:], src[:, kt, hl, tok], w[sl][:, k, :],
                                     start=(kt == 0 and n == 0), stop=(kt == KT - 1 and n == 2))
                    if final and k == KU - 1 and (t, k) != order[-1]:
                        i.then_inc(s_bank, 1)
                i.then_inc(s_pe, 1)

            pe.wait_ge(s_vrow, 32)
            pe.wait_ge(s_ident, 1)
            pe.wait_ge(s_ones, 1)
            T.transpose(ps[7][:, 0:2 * KT], vrow[:], ident[0:2 * KT, 0:2 * KT]).then_inc(s_vt, 1)
            mod_cols(0)
            mod_cols(1)
            norm_turn(0)
            with pe.Fori(2, ADA0) as n:
                mod_cols(n)

            pe.wait_ge(s_lo, 1)
            sh, sl_ = (w[0][:].rearrange("p k n -> p (k n)").rearrange("p (k n) -> p k n", k=KT)
                       for w in (whi, wlo))
            for k in range(KT):
                pe.wait_ge(s_hl, k + 1)
                T.matmul(ps[4][0:CH, :], sh[:, k, :], hT[:, k, :, :], start=(k == 0), stop=False,
                         skip_group_check=True)
                i = T.matmul(ps[4][0:CH, 0:S], sl_[:, k, :], hT[:, k, 0, :], start=False, stop=(k == KT - 1),
                             skip_group_check=True)
            i.then_inc(s_pe, 1)

            def decay_logits():
                pe.wait_ge(s_gl, 1)
                pe.wait_ge(s_wup, 32)
                pe.wait_ge(s_smd, 1)
                pe.wait_ge(s_mod, ADA0)
                for n in range(4):
                    t, a = n // 2, n % 2
                    T.matmul(ps[4 + n][:], gl[:, t * P:t * P + P], wup[:, a, :], start=True,
                             stop=True).then_inc(s_az, 1)

            def forget_turn():
                pe.wait_ge(s_lf, 1)
                pe.wait_ge(s_azd, 4)
                pe.wait_ge(s_aza, 4)
                for t in range(TT):
                    i = T.transpose(ps[7][:, t * FH:t * FH + FH], zm[32:32 + FH, t * P:t * P + P],
                                    ident[32:32 + FH, 32:32 + FH])
                i.then_inc(s_ft, 1)

            def forget_sums():
                pe.wait_ge(s_lft, 1)
                pe.wait_ge(s_mask, 7)
                T.matmul(ps[7][:, 32:48], tri[:], lft[:, 0, :], start=True, stop=True)
                T.matmul(ps[7][:, 48:64], ones[:], lft[:, 0, :], start=True, stop=False)
                T.matmul(ps[7][:, 48:64], tri[:], lft[:, 1, :], start=False, stop=True)
                T.matmul(ps[6][0:FH, 0:P], lft[:, 0, :], tri[:], start=True, stop=True)
                T.matmul(ps[6][0:FH, P:S], lft[:, 0, :], ones[:], start=True, stop=False)
                T.matmul(ps[6][0:FH, P:S], lft[:, 1, :], tri[:], start=False, stop=True).then_inc(s_fc, 1)

            def decay_sums():
                pe.wait_ge(s_la, 1)
                pe.wait_ge(s_fcd, 2)
                lav = la[:].rearrange("p t a n -> p t (a n)")
                for d in range(8):
                    for t in range(TT):
                        o = (d % 2) * S + t * P
                        i = T.matmul(ps[4 + d // 2][:, o:o + P], lav[:, t, d * P:d * P + P], tri16[:],
                                     start=True, stop=True)
                    if d % 2:
                        i.then_inc(s_bt, 1)

            def fox_scores(it, n, j):
                pe.wait_ge(s_evac, events(FOX, it, 10))
                pe.wait_ge(s_rowcum, 16)
                if not (isinstance(n, int) and n == 0):
                    pe.wait_ge(s_S, n * 2)
                for b, (c0, keys) in enumerate(((0, P), (P, S))):
                    T.matmul(ps[4][:, c0:c0 + keys], fq[:, j, b * P:b * P + P], fk[:, j, 0:keys],
                             start=True, stop=False)
                    i = T.matmul(ps[4][:, c0:c0 + keys], ones[0:1, :], ncrow[0:1, bass.ds(n, 1), 0:keys],
                                 start=False, stop=True)
                i.then_inc(s_qk, 1)

            def fox_turn(n, j):
                pe.wait_ge(s_p, n * 2 + 2)
                if not (isinstance(n, int) and n == 0):
                    pe.wait_ge(s_ptc, n)
                for b in range(3):
                    i = T.transpose(ps[5][:, b * P:b * P + P], fs[:, j % 2, b * P:b * P + P], ident[:])
                i.then_inc(s_pt, 1)

            def fox_pv(n, j):
                pe.wait_ge(s_ptc, n + 1)
                if not (isinstance(n, int) and n == 0):
                    pe.wait_ge(s_ob, n * 2)
                v = slice(j * FD, j * FD + FD)
                T.matmul(ps[6][:, 0:P], fv[:, 0, v], pT[:, 0:P], start=True, stop=True)
                T.matmul(ps[6][:, P:S], fv[:, 0, v], pT[:, P:2 * P], start=True, stop=False)
                T.matmul(ps[6][:, P:S], fv[:, 1, v], pT[:, 2 * P:3 * P], start=False, stop=True).then_inc(s_pv, 1)

            def fox_steps(it):
                st = {}
                for j in range(4):
                    n = it * 4 + j
                    st.setdefault(2 * j + 3, []).append(lambda n=n, j=j: fox_pv(n, j))
                for j in range(4):
                    n = it * 4 + j
                    st.setdefault(2 * j + 2, []).append(lambda n=n, j=j: fox_turn(n, j))
                for j in range(4):
                    n = it * 4 + j
                    st.setdefault(2 * j, []).append(lambda n=n, j=j: fox_scores(it, n, j))
                return st

            def gla_scores(h):
                pe.wait_ge(s_qd, h * 5 + 5)
                if not (isinstance(h, int) and h == 0):
                    pe.wait_ge(s_oa, h * 4)
                ch = lambda t_, a, cc: t_[:, a, cc * CH:cc * CH + CH]
                jobs = []
                for cc in range(NC):
                    r0 = (cc % 2) * CH
                    c0 = cc * CH if cc < 2 else 3 * P - 4 * CH + cc * CH
                    jobs.append((r0, c0, ki, cc, lambda a, cc=cc: ch(qd, a, cc)))
                    for q_ in range(cc + 1, NC):
                        c0 = q_ * CH if cc < 2 else 3 * P - 4 * CH + q_ * CH
                        far = q_ - cc
                        if far == 1:
                            rhs = lambda a, q_=q_: ch(qd, a, q_)
                        elif far == 2:
                            rhs = lambda a, q_=q_: qv1[:, a, q_ - 2, :]
                        else:
                            rhs = lambda a: qv2[:, a, :]
                        jobs.append((r0, c0, kd, cc, rhs))
                for r0, c0, keys, cc, rhs in jobs:
                    for a in range(2):
                        i = T.matmul(ps[4][r0:r0 + CH, c0:c0 + CH], ch(keys, a, cc), rhs(a),
                                     start=(a == 0), stop=(a == 1))
                i.then_inc(s_ga, 1)

            def gla_values(h):
                pe.wait_ge(s_am, h * 2 + 2)
                T.matmul(ps[5][:], am[:, 0, :], gv[:, 0, :], start=True, stop=True)
                T.matmul(ps[6][:], am[:, 1, :], gv[:, 0, :], start=True, stop=False)
                T.matmul(ps[6][:], am[:, 2, :], gv[:, 1, :], start=False, stop=True).then_inc(s_go, 1)

            def gla_turn(h):
                for t in range(TT):
                    pe.wait_ge(s_ot, h * 4 + (TT + t + 1))
                    for k in range(4):
                        i = T.transpose(ps[4 + t][:, k * P:k * P + P], ot[:, t, k * P:k * P + P], ident[:])
                    i.then_inc(s_gt, 1)

            def gla_steps(h):
                return {3: [lambda: gla_scores(h)], 5: [lambda: gla_values(h)], 9: [lambda: gla_turn(h)]}

            def merge(*ds):
                out_ = {}
                for d_ in ds:
                    for k_, v_ in d_.items():
                        out_.setdefault(k_, []).extend(v_)
                return out_

            def run(ph, it, steps, unit):
                for g in range(ph["n"]):
                    for step in steps.get(g, ()):
                        step()
                    unit(g)

            def fox(it, steps):
                def unit(g):
                    n = g // UG
                    if n < 2:
                        turned_unit(FOX, it, g, 4 * n, hT, None)
                    else:
                        token_unit(FOX, it, g, 8, hT, 2, None, (-1, 0))
                run(FOX, it, merge(steps, {21: [lambda: mod_cols(ada_no(FOX, it))]}), unit)

            def gla(it, steps):
                def unit(g):
                    n = g // UG
                    if n == 0:
                        token_unit(GLA, it, g, 0, hT, 2, None, (-1, 0) if isinstance(it, int) else (-3, -2))
                    elif n == 1:
                        turned_unit(GLA, it, g, 2, hT, None)
                    else:
                        token_unit(GLA, it, g, 6, hT, 0, None)
                run(GLA, it, merge(steps, {21: [lambda: mod_cols(ada_no(GLA, it))]}), unit)

            def mix(it, steps):
                def unit(g):
                    n = g // UG
                    if g == UG:
                        pe.wait_ge(s_ob, 2 * FH)
                    if g == 3 * UG:
                        pe.wait_ge(s_oa, 4 * 4)
                    turned_unit(MIX, it, g, 4 * n, (hT, obT, hT, oaT)[n], None,
                                (-1, 0, 0, 0) if isinstance(it, int) and n == 0 else (-3, -2, -1, 0))
                run(MIX, it, merge(steps, {12: [lambda: mod_row(ada_no(MIX, it))],
                                           26: [lambda: mod_row(ada_no(MIX, it, 1))]}), unit)

            fox(0, {2: [decay_logits], 4: [forget_turn], 5: [forget_sums], 6: [decay_sums]})
            with pe.Fori(1, 4) as it:
                fox(it, fox_steps(it - 1))
            gla(0, fox_steps(3))
            with pe.Fori(1, 4) as it:
                gla(it, gla_steps(it - 1))
            mix(0, gla_steps(3))
            with pe.Fori(1, 4) as it:
                mix(it, {})
            run(OUT, 0, {}, lambda g: token_unit(
                OUT, 0, g, 2 * (g // UG), hT, 2 * (g // UG % 2),
                (lambda kt: pe.wait_ge(s_cvl, kt // 4 + 1)) if g < UG else None))
            norm_turn(1)

            def ff(it):
                def unit(g):
                    n = g // UG
                    if n < 4:
                        ready = None
                        if n == 0:
                            ready = (lambda kt: pe.wait_ge(s_hl, KT + kt + 1))
                        turned_unit(FF, it, g, 4 * n, obT, ready)
                    else:
                        ready = None
                        if n == 4:
                            ready = (lambda kt: pe.wait_ge(s_actl, it * 16 + (kt + 1)))
                        token_unit(FF, it, g, 8 + 2 * n, oaT, 2 * (n % 2), ready)
                run(FF, it, {}, unit)

            with pe.Fori(0, 4) as it:
                ff(it)


NAMES = ["x", "c", "w_ada", "b_ada", "g_norm1", "w_in", "w_gla_a_up", "b_gla_a", "g_gla_out", "b_fox_f",
         "w_proj_gla", "w_proj_fox", "w_out", "g_norm2", "w_ff1", "w_ff2", "g_final"]


def kernel(**inputs):
    import numpy as np
    import concourse.bacc as bacc
    from concourse.bass_utils import run_bass_kernel_spmd

    nc = bacc.Bacc("TRN2", target_bir_lowering=False, num_devices=1)
    arrays, args = {}, []
    for name in NAMES:
        a = np.ascontiguousarray(inputs[name])
        arrays[f"in_{name}"] = a
        args.append(nc.dram_tensor(f"in_{name}", a.shape, mybir.dt.from_np(a.dtype), kind="ExternalInput").ap())
    args.append(nc.dram_tensor("out_0", (1, S, D), F32, kind="ExternalOutput").ap())
    build(nc, *args)
    r = run_bass_kernel_spmd(nc, [arrays], core_ids=[0])
    return r.results[0]["out_0"]
```

```python
import concourse.bass as bass
from concourse import mybir

F32 = mybir.dt.float32
F32R = mybir.dt.float32r
ACT = mybir.ActivationFunctionType
ALU = mybir.AluOpType
AX_X = mybir.AxisListType.X

P = 128
D = 2048
S = 256
TT = S // P
KT = D // P
NB = 512
KU = 2
UG = KT // KU
LEAD = 3
RING = 4
EPS = 1e-6
BIG = 3.4e38
HK, HV = 256, 512
CH = 64
NC = S // CH
RANK = 16
TAU = 16.0
FH, FD = 16, 128
FSC = FD ** -0.5
GSC = HK ** -0.5

C_GQ, C_GK, C_GV, C_GG, C_LOW = 0, 1024, 2048, 4096, 6144
C_FQ, C_FK, C_FV, C_FL, C_GA, C_GB = 6160, 8208, 10256, 12304, 12320, 14368

FOX = dict(its=4, n=24, ada=[3, 5, 8, 10, 11, 12, 13, 16], ev=10, tr=8, bk=7)
GLA = dict(its=4, n=24, ada=[0, 4, 5, 8, 11, 12, 13, 16], ev=8, tr=4, bk=4)
MIX = dict(its=4, n=32, ada=[0, 1, 2, 4, 5, 8, 10, 11, 13, 14, 16, 17, 18, 20, 21, 24], ev=16, tr=16, bk=12)
OUT = dict(its=1, n=32, ada=[], ev=8, tr=0, bk=4)
FF = dict(its=4, n=64, ada=[], ev=24, tr=16, bk=16)
ADA0 = 8


def lay_out_phases():
    g, u, e, w, a, b = 1, ADA0 * RING, 0, 0, ADA0, 0
    for ph in (FOX, GLA, MIX, OUT, FF):
        ph.update(g0=g, u0=u, e0=e, w0=w, a0=a, b0=b, nu=ph["n"] + len(ph["ada"]), na=len(ph["ada"]) // UG)
        order, pos_g, pos_a = 0, [], []
        for x in range(ph["n"] + LEAD):
            pos_g.append(order)
            order += 1
            slot = x - LEAD
            for s in ph["ada"]:
                if s == slot:
                    pos_a.append(order)
                    order += 1
        assert pos_g[ph["n"]] == ph["nu"] and order == ph["nu"] + LEAD
        ph.update(pos_g=pos_g, pos_a=pos_a)
        g += ph["its"] * ph["n"]
        u += ph["its"] * ph["nu"]
        e += ph["its"] * ph["ev"]
        w += ph["its"] * ph["tr"]
        a += ph["its"] * ph["na"]
        b += ph["its"] * ph["bk"]


lay_out_phases()


def build(nc, x, c, w_ada, b_ada, g_norm1, w_in, w_gla_a_up, b_gla_a, g_gla_out, b_fox_f,
          w_proj_gla, w_proj_fox, w_out, g_norm2, w_ff1, w_ff2, g_final, out):
    base = (nc.sbuf_base + 31) // 32 * 32
    offset = [base]

    def region(size):
        offset[0] += size
        assert offset[0] <= nc.sbuf_usable_end, (offset[0], nc.sbuf_usable_end)
        return offset[0] - size

    def at(name, shape, off, dt=F32):
        return nc.alloc_sbuf_tensor_at(name, shape, dt, offset=off)

    def new(name, shape, dt=F32):
        size = 4
        for n in shape[1:]:
            size *= n
        return at(name, shape, region((size + 31) // 32 * 32), dt)

    raw = [new(f"raw{i}", [P, KU, NB]) for i in range(RING)]
    whi = [new(f"whi{i}", [P, KU, NB], F32R) for i in range(RING)]
    wlo = [new(f"wlo{i}", [P, KU, NB], F32R) for i in range(RING)]
    hT = new("hT", [P, KT, 2, S], F32R)
    ro = region(KT * 2 * S * 4)
    obT = at("obT", [P, KT, 2, S], ro, F32R)
    first = raw + [at(f"first{i}", [P, KU, NB], ro + 4096 * i) for i in range(RING, UG)]
    small = at("small", [P, KT, CH], ro)
    r1 = region(KT * 2 * S * 4)
    oaT = at("oaT", [P, KT, 2, S], r1, F32R)
    x_in = at("x_in", [P, TT, D], r1)
    xT = at("xT", [P, KT, S], r1)
    ncrow = at("ncrow", [1, FH, S], r1)
    xn = at("xn", [P, TT, D], r1 + 16384)
    rm = region(KT * S * 4)
    mT = at("mT", [P, KT, S], rm)
    xl = at("xl", [P, TT, D], rm)
    fq = at("fq", [P, 4, S], rm)
    fk = at("fk", [P, 4, S], rm + 4096)
    fv = at("fv", [P, TT, NB], rm + 8192)
    fs = at("fs", [P, 2, 3 * P], rm + 12288)
    gs = region(12288)
    gq = at("gq", [P, 2, S], gs)
    gk = at("gk", [P, 2, S], gs + 2048)
    gv = at("gv", [P, TT, NB], gs + 4096)
    gg = at("gg", [P, TT, NB], gs + 8192)
    la = at("la", [P, TT, 2, NB], gs)
    gt = region(15360)
    qd = at("qd", [P, 2, S], gt)
    kd = at("kd", [P, 2, S], gt + 2048)
    ep = at("ep", [P, 2, S], gt + 4096)
    ki = at("ki", [P, 2, S], gt + 6144)
    qv1 = at("qv1", [P, 2, 2, CH], gt + 8192)
    qv2 = at("qv2", [P, 2, CH], gt + 9216)
    ot = at("ot", [P, TT, NB], gt + 9728)
    am = at("am", [P, 3, P], gt + 13824)
    wup = at("wup", [RANK + 1, 2, NB], gt)
    tsm = at("tsm", [CH, S], gt + 4096)
    sm = at("sm", [CH, S], gt + 5120)
    zm = at("zm", [CH, S], gt + 6144)
    ab = at("ab", [CH, S], gt + 7168)
    gl = at("gl", [RANK + 1, S], gt + 8192)
    nct = at("nct", [FH, S], gt + 7168)
    tri = at("tri", [P, P], gt + 9216)
    tri16 = at("tri16", [P, P], gt + 9728)
    fm = at("fm", [P, 3 * P], gt + 10240)
    pT = at("pT", [P, 3 * P], gt + 11776)
    lft = at("lft", [P, TT, FH], gt + 13312)
    rb = region(8192)
    bT = at("bT", [P, 8, S], rb)
    lm = at("lm", [P, TT, 2, NB], rb)
    gz = at("gz", [P, 4, S], rb)
    mt = at("mt", [P, 4, S], rb + 4096)
    gfin = at("gfin", [P, D], rb)
    gate1 = at("gate1", [P, D], gs)
    gate2 = at("gate2", [P, D], gs + 8192)
    junk = at("junk", [P, NB], gs)
    t5 = at("t5", [P, 4, S], gs + 16384)
    ident = new("ident", [P, P])
    ones = new("ones", [P, P])
    rmask = region(2 * P * 4)
    mhi = at("mhi", [P, P], rmask)
    mlo = at("mlo", [P, P], rmask + P * 4)
    rdiag = at("rdiag", [P, TT, P], rmask)
    tmp = new("tmp", [P, 2, S])
    acc = new("acc", [P, 2, NB])
    bi = new("bi", [P, NB])
    gout = new("gout", [P, HV])
    modc = new("modc", [P, 4, KT])
    gcol = new("gcol", [P, 2, KT])
    cond = new("cond", [P, KT])
    vrow = at("vrow", [2 * KT, P], gs)
    ctmp = at("ctmp", [P, KT], gs + 512)
    ctm2 = at("ctm2", [P, KT], gs + 576)
    cumc = new("cumc", [P, TT, FH])
    bf = new("bf", [CH, 1])
    neghalf = new("neghalf", [P, 2])
    nst = new("nst", [P, 6, 2])
    nsq = new("nsq", [P, 4, TT])
    fst = new("fst", [P, 2, 6])
    ps = [nc.alloc_psum_tensor(f"ps{i}", [P, 512], F32) for i in range(8)]

    s_go_on = nc.alloc_semaphore("s_go_on")
    s_c = nc.alloc_semaphore("s_c")
    s_vrow = nc.alloc_semaphore("s_vrow")
    s_x = nc.alloc_semaphore("s_x")
    s_gout = nc.alloc_semaphore("s_gout")
    s_wup = nc.alloc_semaphore("s_wup")
    s_bf = nc.alloc_semaphore("s_bf")
    s_bi = nc.alloc_semaphore("s_bi")
    s_rowcum = nc.alloc_semaphore("s_rowcum")
    s_xl = nc.alloc_semaphore("s_xl")
    s_gfin = nc.alloc_semaphore("s_gfin")
    s_out = nc.alloc_semaphore("s_out")
    s_small = nc.alloc_semaphore("s_small")
    s_ident = nc.alloc_semaphore("s_ident")
    s_ones = nc.alloc_semaphore("s_ones")
    s_mask = nc.alloc_semaphore("s_mask")
    s_init = nc.alloc_semaphore("s_init")
    s_vt = nc.alloc_semaphore("s_vt")
    s_gcol = nc.alloc_semaphore("s_gcol")
    s_ce = nc.alloc_semaphore("s_ce")
    s_cd = nc.alloc_semaphore("s_cd")
    s_cond = nc.alloc_semaphore("s_cond")
    s_nss = nc.alloc_semaphore("s_nss")
    s_nsum = nc.alloc_semaphore("s_nsum")
    s_rd = nc.alloc_semaphore("s_rd")
    s_rrow = nc.alloc_semaphore("s_rrow")
    s_xg = nc.alloc_semaphore("s_xg")
    s_ya = nc.alloc_semaphore("s_ya")
    s_nms = nc.alloc_semaphore("s_nms")
    s_ny = nc.alloc_semaphore("s_ny")
    s_nr = nc.alloc_semaphore("s_nr")
    s_xna = nc.alloc_semaphore("s_xna")
    s_xnd = nc.alloc_semaphore("s_xnd")
    s_xt = nc.alloc_semaphore("s_xt")
    s_xte = nc.alloc_semaphore("s_xte")
    s_rowsum = nc.alloc_semaphore("s_rowsum")
    s_row = nc.alloc_semaphore("s_row")
    s_adp = nc.alloc_semaphore("s_adp")
    s_act_on = nc.alloc_semaphore("s_act_on")
    s_acol = nc.alloc_semaphore("s_acol")
    s_ap = nc.alloc_semaphore("s_ap")
    s_hh = nc.alloc_semaphore("s_hh")
    s_hl = nc.alloc_semaphore("s_hl")
    s_hi = nc.alloc_semaphore("s_hi")
    s_lo = nc.alloc_semaphore("s_lo")
    s_pe = nc.alloc_semaphore("s_pe")
    s_ada = nc.alloc_semaphore("s_ada")
    s_modmm = nc.alloc_semaphore("s_modmm")
    s_mod = nc.alloc_semaphore("s_mod")
    s_bank = nc.alloc_semaphore("s_bank")
    s_tmp = nc.alloc_semaphore("s_tmp")
    s_evac = nc.alloc_semaphore("s_evac")
    s_sma = nc.alloc_semaphore("s_sma")
    s_smd = nc.alloc_semaphore("s_smd")
    s_gl = nc.alloc_semaphore("s_gl")
    s_fz = nc.alloc_semaphore("s_fz")
    s_fa = nc.alloc_semaphore("s_fa")
    s_lf = nc.alloc_semaphore("s_lf")
    s_ft = nc.alloc_semaphore("s_ft")
    s_lft = nc.alloc_semaphore("s_lft")
    s_fc = nc.alloc_semaphore("s_fc")
    s_fcd = nc.alloc_semaphore("s_fcd")
    s_az = nc.alloc_semaphore("s_az")
    s_azd = nc.alloc_semaphore("s_azd")
    s_aza = nc.alloc_semaphore("s_aza")
    s_la = nc.alloc_semaphore("s_la")
    s_bt = nc.alloc_semaphore("s_bt")
    s_btd = nc.alloc_semaphore("s_btd")
    s_qk = nc.alloc_semaphore("s_qk")
    s_S = nc.alloc_semaphore("s_S")
    s_max = nc.alloc_semaphore("s_max")
    s_exp = nc.alloc_semaphore("s_exp")
    s_ri = nc.alloc_semaphore("s_ri")
    s_p = nc.alloc_semaphore("s_p")
    s_pt = nc.alloc_semaphore("s_pt")
    s_ptc = nc.alloc_semaphore("s_ptc")
    s_pv = nc.alloc_semaphore("s_pv")
    s_ob = nc.alloc_semaphore("s_ob")
    s_bh = nc.alloc_semaphore("s_bh")
    s_e = nc.alloc_semaphore("s_e")
    s_qd = nc.alloc_semaphore("s_qd")
    s_ga = nc.alloc_semaphore("s_ga")
    s_at = nc.alloc_semaphore("s_at")
    s_am = nc.alloc_semaphore("s_am")
    s_go = nc.alloc_semaphore("s_go")
    s_ss = nc.alloc_semaphore("s_ss")
    s_gms = nc.alloc_semaphore("s_gms")
    s_gy = nc.alloc_semaphore("s_gy")
    s_gnr = nc.alloc_semaphore("s_gnr")
    s_ot = nc.alloc_semaphore("s_ot")
    s_gt = nc.alloc_semaphore("s_gt")
    s_oa = nc.alloc_semaphore("s_oa")
    s_gz = nc.alloc_semaphore("s_gz")
    s_m = nc.alloc_semaphore("s_m")
    s_cvh = nc.alloc_semaphore("s_cvh")
    s_cvl = nc.alloc_semaphore("s_cvl")
    s_x2 = nc.alloc_semaphore("s_x2")
    s_act = nc.alloc_semaphore("s_act")
    s_acth = nc.alloc_semaphore("s_acth")
    s_actl = nc.alloc_semaphore("s_actl")
    s_yo = nc.alloc_semaphore("s_yo")
    s_fraw = [nc.alloc_semaphore(f"s_fraw{i}") for i in range(RING, UG)]
    s_raw = [nc.alloc_semaphore(f"s_raw{i}") for i in range(RING)]

    w_ada_v = w_ada[0].rearrange("(p k) n -> p k n", k=KT)
    w_in_v = w_in[0].rearrange("(k p) n -> p k n", p=P)
    wpa_v = w_proj_gla[0].rearrange("(k p) n -> p k n", p=P)
    wpb_v = w_proj_fox[0].rearrange("(k p) n -> p k n", p=P)
    wo_v = w_out[0].rearrange("(k p) n -> p k n", p=P)
    wf1_v = w_ff1[0].rearrange("(k p) n -> p k n", p=P)
    wf2_v = w_ff2[0].rearrange("(k p) n -> p k n", p=P)
    x_v = x[0].rearrange("(t p) d -> p t d", p=P)
    out_v = out[0].rearrange("(t p) d -> p t d", p=P)

    def small_k(unit):
        return unit[:].rearrange("p k n -> p (k n)").rearrange("p (k n) -> p k n", k=KT)

    def by_head(unit):
        return unit[:].rearrange("p k n -> p (k n)").rearrange("p (k n) -> p k n", k=2 * KU)

    def g_slot(ph, g):
        return (ph["g0"] + g) % RING

    def g_no(ph, it, g):
        return it * ph["n"] + (ph["g0"] + g)

    def u_slot(ph, pos):
        return (ph["u0"] + pos) % RING

    def landed(ph, it, pos):
        return it * (16 * ph["nu"] // RING) + 16 * ((ph["u0"] + pos) // RING + 1)

    def events(ph, it, e=0):
        return it * ph["ev"] + (ph["e0"] + e)

    def turned(ph, it, w=0):
        return it * ph["tr"] + (ph["w0"] + w)

    def bank_done(eng, ph, it, g, b, j, banks):
        if j == banks - 1:
            eng.wait_ge(s_pe, g_no(ph, it, g) + 1)
        else:
            eng.wait_ge(s_bank, it * ph["bk"] + (ph["b0"] + b + j + 1))

    def ada_no(ph, it, a=0):
        return it * ph["na"] + (ph["a0"] + a)

    with nc.Block() as block:

        @block.sync
        def _(sp):
            def load(dst, src, freed, landed_on):
                for sem, count in freed:
                    sp.wait_ge(sem, count)
                    sp.sem_inc(s_go_on, 1)
                sp.dma_start(dst, src).then_inc(landed_on, 16)

            def load_ada(ag, freed, buf, landed_on, mm, col):
                if mm == 0:
                    if isinstance(ag, int) and ag == 0:
                        pass
                    else:
                        sp.wait_ge(s_ada, ag * (2 * UG) - (2 * UG - 2))
                        sp.sem_inc(s_go_on, 1)
                    sp.dma_start(bi[0:1, :], b_ada[0:1, bass.ds(col, NB)]).then_inc(s_bi, 16)
                load(buf[:], w_ada_v[:, KU * mm:KU * mm + KU, bass.ds(col, NB)], freed, landed_on)

            sp.wait_ge(s_small, 1)
            sp.dma_start(small[:, :, 0:RANK], w_in_v[:, :, C_LOW:C_LOW + RANK]).then_inc(s_small, 16)
            sp.dma_start(small[:, :, 32:32 + FH], w_in_v[:, :, C_FL:C_FL + FH]).then_inc(s_small, 16)

            def first_pair(i):
                cols = [sp.snap(i * NB + D), sp.snap(i * NB)] if not isinstance(i, int) else [D, 0]
                for par in range(2):
                    for mm in range(UG):
                        freed = []
                        if not (isinstance(i, int) and par == 0):
                            a = i * (2 * UG) + (UG * par - UG + mm + 1)
                            freed = [(s_ada, a * 2), (s_adp, a)]
                        load_ada(i * 2 + par, freed, first[mm], (s_raw + s_fraw)[mm], mm, cols[par])

            sp.wait_ge(s_init, 1)
            first_pair(0)
            with sp.Fori(1, ADA0 // 2) as i:
                first_pair(i)

            def body(ph, it, source, ada_col):
                src = {}
                for g in range(ph["n"]):
                    src[ph["pos_g"][g]] = ("g", g)
                for k, pos in enumerate(ph["pos_a"]):
                    src[pos] = ("a", k)
                for k in range(1, RING + 1):
                    src[-k] = ("g", -k)
                if ph is FOX and isinstance(it, int):
                    for k in range(1, RING + 1):
                        src[-k] = ("first", (ADA0 - 1) * UG + RING - k)
                for pos in range(ph["nu"]):
                    kind, k = src[pos - RING]
                    if kind == "g":
                        freed = [(s_lo, g_no(ph, it, k) + 1)]
                    elif kind == "a":
                        freed = [(s_ada, ada_no(ph, it, k // UG) * (2 * UG) + 2 * (k % UG + 1))]
                    else:
                        freed = [(s_ada, 2 * (k + 1)), (s_adp, k + 1)]
                    kind, k = src[pos]
                    us = u_slot(ph, pos)
                    if kind == "a":
                        load_ada(ada_no(ph, it, k // UG), freed, raw[us], s_raw[us], k % UG, ada_col[k // UG])
                    else:
                        load(*source(k, us, freed), freed, s_raw[us])

            def phase(ph, make):
                if ph["its"] == 1:
                    body(ph, 0, *make(0))
                    return
                if ph is FOX:
                    body(ph, 0, *make(0))
                with sp.Fori(1 if ph is FOX else 0, ph["its"]) as it:
                    body(ph, it, *make(it))

            def snap(v):
                return v if isinstance(v, int) else sp.snap(v)

            def fox(it):
                cols = [snap(it * NB + cc) for cc in (C_FQ, C_FK, C_FV)]
                return (lambda g, us, _: (raw[us][:], w_in_v[:, KU * (g % UG):KU * (g % UG) + KU,
                                                    bass.ds(cols[g // UG], NB)]),
                        [snap(it * NB + 3 * D)])

            def gla(it):
                qk = [snap(it * HK + C_GQ), snap(it * HK + C_GK)]
                cols = [None, snap(it * NB + C_GG), snap(it * NB + C_GV)]

                def source(g, us, freed):
                    r = raw[us]
                    ks = slice(KU * (g % UG), KU * (g % UG) + KU)
                    if g < UG:
                        return by_head(r), w_in_v[:, 4 * (g % 4):4 * (g % 4) + 4, bass.ds(qk[g // 4], HK)]
                    return r[:], w_in_v[:, ks, bass.ds(cols[g // UG], NB)]
                return source, [snap(it * NB + 4 * D)]

            def mix(it):
                n0 = snap(it * NB)
                cols = [snap(it * NB + C_GB), n0, snap(it * NB + C_GA), n0]
                views = [w_in_v, wpb_v, w_in_v, wpa_v]
                return (lambda g, us, _: (raw[us][:], views[g // UG][:, KU * (g % UG):KU * (g % UG) + KU,
                                                            bass.ds(cols[g // UG], NB)]),
                        [snap(it * NB + 2 * D), snap(it * NB + 5 * D)])

            def wout(it):
                return (lambda g, us, _: (raw[us][:], wo_v[:, KU * (g % UG):KU * (g % UG) + KU,
                                                  NB * (g // UG):NB * (g // UG) + NB]), [])

            def ff(it):
                cols = [snap(it * D + NB * n) for n in range(4)]
                rows = [snap(it * KT + KU * n) for n in range(UG)]

                def source(g, us, freed):
                    r = raw[us]
                    if g < 4 * UG:
                        return r[:], wf1_v[:, KU * (g % UG):KU * (g % UG) + KU, bass.ds(cols[g // UG], NB)]
                    n = g // UG - 4
                    return r[:], wf2_v[:, bass.ds(rows[g % UG], KU), NB * n:NB * n + NB]
                return source, []

            phase(FOX, fox)
            phase(GLA, gla)
            phase(MIX, mix)
            phase(OUT, wout)
            phase(FF, ff)
            for h in range(2):
                half = slice(h * (D // 2), (h + 1) * (D // 2))
                for t, done in enumerate((s_yo, s_ya)):
                    sp.wait_ge(done, h + 1)
                    sp.dma_start(out_v[:, t, half], xl[:, t, half]).then_inc(s_out, 16)
            sp.wait_ge(s_out, 16 * 2 * TT)

        @block.gpsimd
        def _(pool):
            nc.gpsimd.memset(small[:], 0.0).then_inc(s_small, 1)
            nc.gpsimd.memset(bi[:], 0.0).then_inc(s_init, 1)
            nc.gpsimd.memset(ident[:], 0.0)
            nc.gpsimd.memset(ones[:], 1.0).then_inc(s_ones, 1)
            nc.gpsimd.memset(neghalf[:], -0.5)
            nc.gpsimd.memset(mhi[:], BIG)
            nc.gpsimd.memset(mlo[:], -BIG)
            nc.gpsimd.memset(tri[:], 1.0)
            nc.gpsimd.memset(tri16[:], 1.0 / TAU)
            nc.gpsimd.memset(fm[:], 0.0)
            nc.gpsimd.memset(am[:], 0.0)
            nc.gpsimd.memset(gl[:], 1.0).then_inc(s_init, 1)
            pool.wait_ge(s_init, 2)
            nc.gpsimd.affine_select(out=ident[:], in_=ident[:], compare_op=ALU.not_equal, fill=1.0, base=0,
                                    pattern=[[-1, P]], channel_multiplier=1).then_inc(s_ident, 1)
            for t_ in (mhi, mlo, tri, tri16):
                nc.gpsimd.affine_select(out=t_[:], in_=t_[:], compare_op=ALU.is_ge, fill=0.0, base=0,
                                        pattern=[[1, P]], channel_multiplier=-1).then_inc(s_mask, 1)
            for b in (0, 2):
                nc.gpsimd.affine_select(out=fm[:, b * P:b * P + P], in_=fm[:, b * P:b * P + P],
                                        compare_op=ALU.is_ge, fill=-1e30, base=0,
                                        pattern=[[-1, P]], channel_multiplier=1).then_inc(s_mask, 1)
            pool.wait_ge(s_mask, 6)
            nc.gpsimd.memset(tri16[0:CH, CH:P], 0.0).then_inc(s_mask, 1)

            def norm_pow(r):
                pool.wait_ge(s_nms, r + 1)
                nc.gpsimd.tensor_tensor(nst[:, 2, :], nst[:, 1, :], neghalf[:], ALU.pow).then_inc(s_ny, 1)

            norm_pow(0)
            pool.wait_ge(s_fcd, 2)
            nc.gpsimd.dma_start(ncrow[0:1, :, :], nct[:]).then_inc(s_rowcum, 16)
            with pool.Fori(0, 4) as h:
                pool.wait_ge(s_gms, h + 1)
                nc.gpsimd.tensor_tensor(nst[:, 2, :], nst[:, 1, :], neghalf[:], ALU.pow).then_inc(s_gy, 1)
            norm_pow(1)
            norm_pow(2)

        @block.scalar
        def _(act):
            act.dma_start(cond[:], c[0].rearrange("(p k) -> p k", k=KT)).then_inc(s_c, 16)
            act.dma_start(vrow[0:KT, :], g_norm1[0].rearrange("(k n) -> k n", n=P)).then_inc(s_vrow, 16)
            act.dma_start(vrow[KT:2 * KT, :], g_norm2[0].rearrange("(k n) -> k n", n=P)).then_inc(s_vrow, 16)
            act.dma_start(x_in[:], x_v).then_inc(s_x, 16)
            act.dma_start(gout[:], g_gla_out[0].partition_broadcast(P)).then_inc(s_gout, 16)
            act.dma_start(wup[0:RANK, :, :], w_gla_a_up[0].rearrange("r (a n) -> r a n", n=NB)).then_inc(s_wup, 16)
            act.dma_start(wup[RANK:RANK + 1, :, :], b_gla_a[0:1].rearrange("r (a n) -> r a n", n=NB)).then_inc(s_wup, 16)
            act.dma_start(bf[32:32 + FH, :], b_fox_f[0].rearrange("(h a) -> h a", a=1)).then_inc(s_bf, 16)
            act.wait_ge(s_c, 16)
            nc.scalar.activation(ctmp[:], cond[:], ACT.Exp, scale=-1.0).then_inc(s_ce, 1)

            def norm_squares():
                for t in range(TT):
                    nc.scalar.activation(xn[:, t, :], x_in[:, t, :], ACT.Square,
                                         accum_out=nst[:, 0, t:t + 1]).then_inc(s_nss, 1)

            def part_squares(r, n, x2, squares):
                for t in range(TT):
                    act.wait_ge(s_x2, x2 + t + 1)
                    act.wait_ge(s_nss, 2 + 8 * (r - 1) + 2 * n + t)
                    nc.scalar.activation(squares, xl[:, t, n * NB:(n + 1) * NB], ACT.Square,
                                         accum_out=nsq[:, n, t:t + 1]).then_inc(s_nss, 1)

            def x2_evac(n):
                for t in range(TT):
                    act.wait_ge(s_xt, 8 + 2 * n + t + 1)
                    nc.scalar.activation(xT[:, 4 * n:4 * n + 4, t * P:t * P + P],
                                         ps[4 + t][:].rearrange("p (k n) -> p k n", k=4),
                                         ACT.Copy).then_inc(s_xte, 1)

            def norm_rows(r, src):
                act.wait_ge(s_nr, 4 * r + 4)
                nc.scalar.activation(xn[:, 1, :], src[:, 1, :], ACT.Copy,
                                     scale=nst[:, 5, 1:2]).then_inc(s_xna, 1)

            def norm_evac(r):
                act.wait_ge(s_xna, r + 1)
                for n in range(8):
                    t, b = n // 4, n % 4
                    act.wait_ge(s_xt, 8 * r + n + 1)
                    nc.scalar.activation(xT[:, 4 * b:4 * b + 4, t * P:t * P + P],
                                         ps[b][:].rearrange("p (k n) -> p k n", k=4),
                                         ACT.Copy).then_inc(s_xte, 1)

            def row_first(i, par):
                act.wait_ge(s_rowsum, i * 2 + (par + 1))
                if not (isinstance(i, int) and par == 0):
                    act.wait_ge(s_modmm, i * 2 + par)
                nc.scalar.activation(tmp[0:1, :, :].rearrange("p a n -> p (a n)"), ps[6 + par][0:1, :],
                                     ACT.Copy).then_inc(s_row, 1)

            def norm1_split(i):
                for k in range(4):
                    kt = i * 4 + k
                    act.wait_ge(s_ap, kt + 1)
                    if isinstance(i, int):
                        nc.scalar.activation(hT[:, kt, 0, :], xT[:, kt, :], ACT.Copy).then_inc(s_hh, 1)
                    else:
                        act.sem_inc(s_act_on, 1)
                        nc.scalar.activation(hT[:, bass.ds(kt, 1), 0, :], xT[:, bass.ds(kt, 1), :],
                                             ACT.Copy).then_inc(s_hh, 1)

            def prep(ph, it, g):
                pos = ph["pos_g"][g]
                us, gs_ = u_slot(ph, pos), g_slot(ph, g)
                act.wait_ge(s_raw[us], landed(ph, it, pos))
                act.wait_ge(s_pe, g_no(ph, it, g) - (RING - 1))
                nc.scalar.activation(whi[gs_][:], raw[us][:], ACT.Copy).then_inc(s_hi, 1)

            def turn(ph, it, g, e, b, scale=1.0, banks=(0, 1, 2, 3)):
                for j, bank in enumerate(banks):
                    bank_done(act, ph, it, g, b, j, len(banks))
                    need = events(ph, it, e) if j == 0 else events(ph, it, e + j - 1)
                    if not (isinstance(need, int) and need <= 0):
                        act.wait_ge(s_evac, need)
                    nc.scalar.activation(tmp[:, j % 2, :], ps[bank][:, S:2 * S], ACT.Copy,
                                         scale=scale).then_inc(s_tmp, 1)

            def fox_exp(n, j):
                act.wait_ge(s_max, 2 * n + 2)
                for b, sl in enumerate((slice(0, P), slice(P, 3 * P))):
                    nc.scalar.activation(fs[:, j % 2, sl], fs[:, j % 2, sl], ACT.Exp,
                                         bias=fst[:, j % 2, b:b + 1],
                                         accum_out=fst[:, j % 2, 2 + b:3 + b]).then_inc(s_exp, 1)

            def fox_norm(n, j):
                act.wait_ge(s_ri, n + 1)
                for b, sl in enumerate((slice(0, P), slice(P, 3 * P))):
                    nc.scalar.activation(fs[:, j % 2, sl], fs[:, j % 2, sl], ACT.Copy,
                                         scale=fst[:, j % 2, 4 + b:5 + b]).then_inc(s_p, 1)

            def fox_turned(n, j):
                act.wait_ge(s_pt, n + 1)
                if not (isinstance(n, int) and n == 0):
                    act.wait_ge(s_pv, n)
                nc.scalar.activation(pT[:], ps[5][:, 0:3 * P], ACT.Copy).then_inc(s_ptc, 1)

            def gla_exps(h):
                act.wait_ge(s_bh, 2 * h + 1)
                nc.scalar.activation(ep[:], qd[:], ACT.Exp).then_inc(s_e, 1)
                nc.scalar.activation(ki[:], qd[:], ACT.Exp, scale=-1.0).then_inc(s_e, 1)
                act.wait_ge(s_bh, 2 * h + 2)
                nc.scalar.activation(kd[:], kd[:], ACT.Exp).then_inc(s_e, 1)

            def gla_attn(h):
                act.wait_ge(s_ga, h + 1)
                if not (isinstance(h, int) and h == 0):
                    act.wait_ge(s_go, h)
                a3 = ps[4][:, 0:3 * P]
                amf = am[:].rearrange("p a n -> p (a n)")
                for p0, p1, c0, c1 in ((0, CH, 0, 3 * P), (CH, P, CH, 2 * P), (CH, P, 2 * P + CH, 3 * P)):
                    nc.scalar.activation(amf[p0:p1, c0:c1], a3[p0:p1, c0:c1], ACT.Copy).then_inc(s_at, 1)

            def gla_squares(h):
                act.wait_ge(s_go, h + 1)
                if not (isinstance(h, int) and h == 0):
                    act.wait_ge(s_gt, 2 * h)
                for t in range(TT):
                    nc.scalar.activation(ot[:, t, :], ps[5 + t][:], ACT.Square,
                                         accum_out=nst[:, 0, t:t + 1]).then_inc(s_ss, 1)

            def take(ph, it, g, b, banks, dst, func, used, each):
                if not isinstance(it, int):
                    act.wait_ge(used, it * each)
                for t in range(TT):
                    bank_done(act, ph, it, g, b, t, TT)
                    nc.scalar.activation(dst[:, t, :], ps[banks + t][:], func).then_inc(s_evac, 1)

            def gate_sigmoid(it, e):
                act.wait_ge(s_evac, events(MIX, it, e))
                nc.scalar.activation(gz[:], gz[:], ACT.Sigmoid).then_inc(s_gz, 1)

            def run(ph, it, steps, last=None, early=()):
                for g in range(ph["n"]):
                    for step in steps.get(g, ())[:1] if g in early else ():
                        step()
                    if g + LEAD < (last or ph["n"] + LEAD):
                        prep(ph, it, g + LEAD)
                    for step in steps.get(g, ())[1 if g in early else 0:]:
                        step()

            act.wait_ge(s_small, 33)
            nc.scalar.activation(small_k(whi[0]), small[:], ACT.Copy).then_inc(s_hi, 1)
            act.wait_ge(s_x, 16)
            norm_squares()
            row_first(0, 0)
            norm_rows(0, x_in)
            norm_evac(0)
            row_first(0, 1)
            with act.Fori(1, ADA0 // 2) as i:
                norm1_split(i - 1)
                for par in range(2):
                    row_first(i, par)
            norm1_split(ADA0 // 2 - 1)
            for g in range(LEAD):
                act.wait_ge(s_raw[u_slot(FOX, g)], landed(FOX, 0, g))
                nc.scalar.activation(whi[g_slot(FOX, g)][:], raw[u_slot(FOX, g)][:], ACT.Copy).then_inc(s_hi, 1)

            def small_turn():
                act.wait_ge(s_pe, 1)
                nc.scalar.activation(tsm[:], ps[4][0:CH, S:2 * S], ACT.Copy).then_inc(s_sma, 1)

            def small_log():
                f = slice(32, 32 + FH)
                act.wait_ge(s_fz, 1)
                nc.scalar.activation(ab[f, :], sm[f, :], ACT.Abs).then_inc(s_fa, 1)
                act.wait_ge(s_fa, 1)
                nc.scalar.activation(ab[f, :], ab[f, :], ACT.Exp, scale=-1.0).then_inc(s_fa, 1)

            def decay_abs():
                for n in range(4):
                    act.wait_ge(s_az, n + 1)
                    nc.scalar.activation(la[:, n // 2, n % 2, :], ps[4 + n][:], ACT.Abs).then_inc(s_aza, 1)
                act.wait_ge(s_aza, 4)
                nc.scalar.activation(la[:], la[:], ACT.Exp, scale=-1.0).then_inc(s_aza, 1)

            def logs():
                f = slice(32, 32 + FH)
                act.wait_ge(s_fa, 2)
                nc.scalar.activation(ab[f, :], ab[f, :], ACT.Ln, bias=1.0).then_inc(s_fa, 1)
                act.wait_ge(s_aza, 5)
                nc.scalar.activation(la[:], la[:], ACT.Ln, bias=1.0).then_inc(s_aza, 1)

            def decay_evac():
                for b in range(4):
                    act.wait_ge(s_bt, b + 1)
                    nc.scalar.activation(bT[:, 2 * b:2 * b + 2, :],
                                         ps[4 + b][:].rearrange("p (a n) -> p a n", a=2),
                                         ACT.Copy).then_inc(s_btd, 1)

            def fox_steps(it):
                st = {}
                for j in range(4):
                    n = it * 4 + j
                    st.setdefault(2 * j, []).append(lambda n=n, j=j: fox_exp(n, j))
                    st.setdefault(2 * j + 1, []).append(lambda n=n, j=j: fox_norm(n, j))
                    st.setdefault(2 * j + 3, []).append(lambda n=n, j=j: fox_turned(n, j))
                return st

            def gla_steps(h):
                return {0: [lambda: gla_exps(h)], 3: [lambda: gla_attn(h)], 5: [lambda: gla_squares(h)]}

            def merge(*ds):
                out_ = {}
                for d_ in ds:
                    for k_, v_ in d_.items():
                        out_.setdefault(k_, []).extend(v_)
                return out_

            def fox_gemm(it):
                return {7: [lambda: turn(FOX, it, 7, 0, 0, FSC)], 15: [lambda: turn(FOX, it, 15, 4, 3)],
                        23: [lambda: take(FOX, it, 23, 6, 0, fv, ACT.Copy, s_pv, 4)]}

            def gla_gemm(it):
                return {3: [lambda: turn(GLA, it, 3, 0, 0, GSC, (0, 1))],
                        7: [lambda: turn(GLA, it, 7, 2, 1, 1.0, (2, 3))],
                        15: [lambda: take(GLA, it, 15, 2, 0, gg, ACT.Silu, s_ot, 4)],
                        23: [lambda: take(GLA, it, 23, 3, 2, gv, ACT.Copy, s_go, 1)]}

            def mix_gemm(it):
                return {7: [lambda: turn(MIX, it, 7, 0, 0), lambda: gate_sigmoid(it, 4)],
                        15: [lambda: turn(MIX, it, 15, 4, 3)],
                        23: [lambda: turn(MIX, it, 23, 8, 6), lambda: gate_sigmoid(it, 12)],
                        31: [lambda: turn(MIX, it, 31, 12, 9)]}

            run(FOX, 0, merge(fox_gemm(0), {0: [small_turn], 1: [small_log], 2: [decay_abs], 3: [logs],
                                            6: [decay_evac]}))
            with act.Fori(1, 4) as it:
                run(FOX, it, merge(fox_steps(it - 1), fox_gemm(it)))
            run(GLA, 0, merge(fox_steps(3), gla_gemm(0)))
            with act.Fori(1, 4) as it:
                run(GLA, it, merge(gla_steps(it - 1), gla_gemm(it)))
            run(MIX, 0, merge(gla_steps(3), mix_gemm(0)), early=(7, 15, 23, 31))
            with act.Fori(1, 3) as it:
                run(MIX, it, mix_gemm(it), early=(7, 15, 23, 31))

            def merged_hi(b):
                nc.scalar.activation(hT[:, 4 * b:4 * b + 4, 0, :], mT[:, 4 * b:4 * b + 4, :],
                                     ACT.Copy).then_inc(s_cvh, 1)

            def merged_first():
                act.wait_ge(s_pe, g_no(MIX, 3, 3 * UG))
                act.wait_ge(s_m, 3 * 3)
                merged_hi(0)

            run(MIX, 3, merge(mix_gemm(3), {25: [merged_first], 26: [lambda: merged_hi(1)],
                                            27: [lambda: merged_hi(2)]}), early=(7, 15, 23, 31))
            act.wait_ge(s_m, 3 * 4)
            merged_hi(3)

            def out_loads():
                act.wait_ge(s_cvl, 4)
                act.dma_start(xl[:], x_v).then_inc(s_xl, 16)
                act.dma_start(gfin[:], g_final.partition_broadcast(P)).then_inc(s_gfin, 16)

            st = {0: [out_loads]}
            for n in range(3):
                st[UG * n + UG] = st.get(UG * n + UG, []) + [lambda n=n: part_squares(1, n, 2 * n, xn[:, 0, 0:NB])]
                st[UG * n + UG + 3] = [lambda n=n: x2_evac(n)]
            run(OUT, 0, st)
            part_squares(1, 3, 6, xn[:, 0, 0:NB])
            x2_evac(3)
            for k in range(KT):
                act.wait_ge(s_ap, KT + k + 1)
                nc.scalar.activation(obT[:, k, 0, :], xT[:, k, :], ACT.Identity,
                                     bias=modc[:, 2, k:k + 1]).then_inc(s_hh, 1)

            def ff_hi(it, n):
                act.wait_ge(s_act, it * 4 + (n + 1))
                nc.scalar.activation(oaT[:, 4 * n:4 * n + 4, 0, :], t5[:], ACT.Copy).then_inc(s_acth, 1)

            def ff_steps(it):
                st = {}
                for n in range(4):
                    st[UG * n + UG - 1] = [lambda n=n: turn(FF, it, UG * n + UG - 1, 4 * n, 3 * n)]
                    st[UG * n + UG] = [lambda n=n: ff_hi(it, n)]
                return st

            with act.Fori(0, 3) as it:
                run(FF, it, ff_steps(it))
            run(FF, 3, merge(ff_steps(3), {UG * (4 + n) + UG: [lambda n=n: part_squares(2, n, 32 + 2 * n, junk[:])]
                                           for n in range(3)}), last=FF["n"])

            part_squares(2, 3, 32 + 6, junk[:])
            act.wait_ge(s_nr, 12)
            act.wait_ge(s_xg, 4)
            for h in range(2):
                half = slice(h * (D // 2), (h + 1) * (D // 2))
                nc.scalar.activation(xl[:, 1, half], xl[:, 1, half], ACT.Copy,
                                     scale=nst[:, 5, 1:2]).then_inc(s_ya, 1)

        @block.vector
        def _(dve):
            V = nc.vector

            dve.wait_ge(s_ce, 1)
            V.tensor_scalar(ctm2[:], ctmp[:], 1.0, None, ALU.add).then_inc(s_cd, 1)
            dve.wait_ge(s_cd, 1)
            V.reciprocal(ctmp[:], ctm2[:]).then_inc(s_cd, 1)
            dve.wait_ge(s_cd, 2)
            V.tensor_tensor(cond[:], cond[:], ctmp[:], ALU.mult).then_inc(s_cond, 1)
            dve.wait_ge(s_vt, 1)
            V.tensor_copy(gcol[:], ps[3][:, 0:2 * KT].rearrange("p (a k) -> p a k", a=2)).then_inc(s_gcol, 1)
            dve.wait_ge(s_cond, 1)

            def ada(ag, mm, us, count):
                dve.wait_ge(s_raw[us], count)
                if mm == 0:
                    dve.wait_ge(s_bi, ag * 16 + 16)
                    if not (isinstance(ag, int) and ag == 0):
                        dve.wait_ge(s_modmm, ag)
                else:
                    dve.wait_ge(s_ada, ag * (2 * UG) + 2 * mm)
                for h in range(2):
                    k = 2 * mm + h
                    if k == 1:
                        i = V.tensor_scalar(acc[:, h, :], raw[us][:, h, :], cond[:, k:k + 1], None, ALU.mult)
                    else:
                        i = V.scalar_tensor_tensor(acc[:, h, :], raw[us][:, h, :], cond[:, k:k + 1],
                                                   bi[:] if k == 0 else acc[:, h, :], ALU.mult, ALU.add)
                    i.then_inc(s_ada, 1)

            def mod_cols(ag, col):
                dve.wait_ge(s_modmm, ag + 1)
                flat = modc[:].rearrange("p a k -> p (a k)")
                V.tensor_scalar(flat[:, bass.ds(col, 4)], ps[7][:, 0:4], 1.0, None, ALU.mult).then_inc(s_mod, 1)

            def mod_row(ag, dst, col):
                dve.wait_ge(s_modmm, ag + 1)
                V.tensor_scalar(dst[:, bass.ds(col, NB)], ps[7][:], 1.0, None, ALU.mult).then_inc(s_mod, 1)

            def norm_mean(count, s_in, out_sem, n):
                dve.wait_ge(s_in, count)
                V.tensor_scalar(nst[:, 1, :], nst[:, 0, :], 1.0 / n, EPS, ALU.mult, ALU.add).then_inc(out_sem, 1)

            def newton(s_seed, count, s_own, before):
                y, t1, t2, r_ = (nst[:, n, :] for n in (2, 3, 4, 5))
                dve.wait_ge(s_seed, count)
                V.tensor_tensor(t1, y, y, ALU.mult).then_inc(s_own, 1)
                dve.wait_ge(s_own, before + 1)
                V.tensor_tensor(t2, t1, nst[:, 1, :], ALU.mult).then_inc(s_own, 1)
                dve.wait_ge(s_own, before + 2)
                V.tensor_scalar(t1, t2, -0.5, 1.5, ALU.mult, ALU.add).then_inc(s_own, 1)
                dve.wait_ge(s_own, before + 3)
                V.tensor_tensor(r_, y, t1, ALU.mult).then_inc(s_own, 1)
                dve.wait_ge(s_own, before + 4)

            def norm_rows(r, src):
                newton(s_ny, r + 1, s_nr, 4 * r)
                V.tensor_scalar(xn[:, 0, :], src[:, 0, :], nst[:, 5, 0:1], None, ALU.mult).then_inc(s_xnd, 1)

            def part_sums(r):
                dve.wait_ge(s_nss, 2 + 8 * r)
                V.tensor_reduce(nst[:, 0, :], nsq[:].rearrange("p n t -> p t n"), AX_X, ALU.add).then_inc(s_nsum, 1)
                norm_mean(r, s_nsum, s_nms, D)

            def norm2():
                part_sums(1)
                newton(s_ny, 2, s_nr, 4)
                for t in range(TT):
                    V.tensor_scalar(rdiag[:, t, :], ident[:], nst[:, 5, t:t + 1], None, ALU.mult).then_inc(s_rd, 1)
                dve.wait_ge(s_rrow, 1)
                dve.wait_ge(s_acol, 5)
                for k in range(KT + 1):
                    if k < KT:
                        if k == 0 or k == 12:
                            dve.wait_ge(s_xte, 14 if k == 0 else 16)
                        V.scalar_tensor_tensor(xT[:, k, :], xT[:, k, :], gcol[:, 1, k:k + 1], ps[6][:, 0:S],
                                               ALU.mult, ALU.mult).then_inc(s_ap, 1)
                    if k > 0:
                        dve.wait_ge(s_hh, KT + k)
                        V.scalar_tensor_tensor(obT[:, k - 1, 1, :], xT[:, k - 1, :], modc[:, 2, k - 1:k],
                                               obT[:, k - 1, 0, :].bitcast(F32), ALU.add,
                                               ALU.subtract).then_inc(s_hl, 1)

            def lo(count, us, gs_):
                dve.wait_ge(s_hi, count)
                V.tensor_tensor(wlo[gs_][:], raw[us][:], whi[gs_][:].bitcast(F32),
                                ALU.subtract).then_inc(s_lo, 1)

            def prep(ph, it, g):
                lo(g_no(ph, it, g) + 1, u_slot(ph, ph["pos_g"][g]), g_slot(ph, g))

            def ada_first(i, par, mm):
                n = i * 2 + par
                dve.wait_ge((s_raw + s_fraw)[mm], i * 32 + 16 * (par + 1))
                if mm == 0:
                    dve.wait_ge(s_bi, n * 16 + 16)
                    if not isinstance(i, int):
                        dve.wait_ge(s_modmm, n - 1)
                else:
                    dve.wait_ge(s_ada, n * (2 * UG) + 2 * mm)
                V.scalar_tensor_tensor(acc[:, par, :], first[mm][:, 0, :], cond[:, 2 * mm:2 * mm + 1],
                                       bi[:] if mm == 0 else acc[:, par, :], ALU.mult, ALU.add).then_inc(s_ada, 2)

            def mod_first(i, par):
                dve.wait_ge(s_modmm, i * 2 + (par + 1))
                flat = modc[:].rearrange("p a k -> p (a k)")
                V.tensor_scalar(flat[:, bass.ds(i * 4 + (0 if par else KT), 4)], ps[4 + par][:, 0:4],
                                1.0, None, ALU.mult).then_inc(s_mod, 1)

            def norm1_cols(i):
                blk = bass.ds(i * 4, 4)
                dve.wait_ge(s_mod, i * 2 + 2)
                V.scalar_tensor_tensor(gcol[:, 0, blk], modc[:, 1, blk], 1.0, gcol[:, 0, blk],
                                       ALU.add, ALU.mult).then_inc(s_acol, 1)
                dve.wait_ge(s_acol, i + 1)

            def norm1_apply(i, k):
                kt = i * 4 + k
                row = xT[:, bass.ds(kt, 1), :]
                V.tensor_scalar(row, row, gcol[:, 0, bass.ds(kt, 1)], modc[:, 0, bass.ds(kt, 1)],
                                ALU.mult, ALU.add).then_inc(s_ap, 1)

            def norm1_lo(i, k):
                kt = i * 4 + k
                dve.wait_ge(s_hh, kt + 1)
                V.tensor_tensor(hT[:, bass.ds(kt, 1), 1, :], xT[:, bass.ds(kt, 1), :],
                                hT[:, bass.ds(kt, 1), 0, :].bitcast(F32), ALU.subtract).then_inc(s_hl, 1)

            def first_pair(i):
                for par in range(2):
                    for mm in range(UG):
                        ada_first(i, par, mm)
                        if isinstance(i, int):
                            if (par, mm) == (0, 6):
                                norm_mean(2, s_nss, s_nms, D)
                            if (par, mm) == (1, 0):
                                norm_rows(0, x_in)
                        else:
                            k = UG * par + mm - 5
                            if k == -1:
                                mod_first(i - 1, 1)
                                norm1_cols(i - 1)
                                dve.wait_ge(s_xte, 8)
                            if 0 <= k < 4:
                                norm1_apply(i - 1, k)
                            if 1 <= k < 5:
                                norm1_lo(i - 1, k - 1)
                        if par == 1 and mm == 4:
                            mod_first(i, 0)
                        if isinstance(i, int) and (par, mm) == (0, 2):
                            dve.wait_ge(s_hi, 1)
                            V.tensor_tensor(small_k(wlo[0]), small[:], small_k(whi[0]).bitcast(F32),
                                            ALU.subtract).then_inc(s_lo, 1)

            first_pair(0)
            with dve.Fori(1, ADA0 // 2) as i:
                first_pair(i)
            last = ADA0 // 2 - 1
            mod_first(last, 1)
            norm1_cols(last)
            for k in range(5):
                if k < 4:
                    norm1_apply(last, k)
                if k > 0:
                    norm1_lo(last, k - 1)
            for g in range(LEAD):
                lo(g + 2, u_slot(FOX, g), g_slot(FOX, g))

            def run(ph, it, steps, last=None):
                ada_at = {s_: k for k, s_ in enumerate(ph["ada"])}
                for g in range(ph["n"]):
                    for step in steps.get(g, ()):
                        step()
                    if g + LEAD < (last or ph["n"] + LEAD):
                        prep(ph, it, g + LEAD)
                    if g in ada_at:
                        k = ada_at[g]
                        pos = ph["pos_a"][k]
                        ada(ada_no(ph, it, k // UG), k % UG, u_slot(ph, pos), landed(ph, it, pos))

            def join(ph, it, e, w, dst, scale=1.0, banks=(0, 1, 2, 3)):
                for j, bank in enumerate(banks):
                    dve.wait_ge(s_tmp, turned(ph, it, w + j) + 1)
                    if scale == 1.0:
                        i = V.tensor_tensor(dst(j), ps[bank][:, 0:S], tmp[:, j % 2, :], ALU.add)
                    else:
                        i = V.scalar_tensor_tensor(dst(j), ps[bank][:, 0:S], scale, tmp[:, j % 2, :],
                                                   ALU.mult, ALU.add)
                    i.then_inc(s_evac, 1)

            f = slice(32, 32 + FH)

            def small_join():
                dve.wait_ge(s_sma, 1)
                V.tensor_tensor(sm[:], ps[4][0:CH, 0:S], tsm[:], ALU.add).then_inc(s_smd, 1)
                dve.wait_ge(s_smd, 1)
                dve.wait_ge(s_init, 2)
                V.tensor_copy(gl[0:RANK, :], sm[0:RANK, :]).then_inc(s_gl, 1)
                dve.wait_ge(s_bf, 16)
                V.tensor_scalar(sm[f, :], sm[f, :], bf[f, 0:1], None, ALU.add).then_inc(s_fz, 1)
                dve.wait_ge(s_fz, 1)
                V.tensor_scalar(zm[f, :], sm[f, :], 0.0, None, ALU.min).then_inc(s_fz, 1)

            def decay_min():
                for n in range(4):
                    dve.wait_ge(s_aza, n + 1)
                    V.tensor_scalar(lm[:, n // 2, n % 2, :], ps[4 + n][:], 0.0, None, ALU.min).then_inc(s_azd, 1)

            def log_sigmoids():
                dve.wait_ge(s_fa, 3)
                dve.wait_ge(s_fz, 2)
                V.tensor_tensor(zm[f, :], zm[f, :], ab[f, :], ALU.subtract).then_inc(s_lf, 1)
                dve.wait_ge(s_aza, 6)
                dve.wait_ge(s_azd, 4)
                V.tensor_tensor(la[:], lm[:], la[:], ALU.subtract).then_inc(s_la, 1)

            def forget_cols():
                dve.wait_ge(s_ft, 1)
                V.tensor_copy(lft[:], ps[7][:, 0:TT * FH].rearrange("p (t h) -> p t h", t=TT)).then_inc(s_lft, 1)

            def forget_cums():
                dve.wait_ge(s_fc, 1)
                V.tensor_copy(cumc[:], ps[7][:, 32:32 + TT * FH].rearrange("p (t h) -> p t h", t=TT)
                              ).then_inc(s_fcd, 1)
                V.tensor_scalar(nct[:], ps[6][0:FH, 0:S], -1.0, None, ALU.mult).then_inc(s_fcd, 1)

            halves = (slice(0, P), slice(P, 3 * P))

            def fox_scores(n, j):
                dve.wait_ge(s_qk, n + 1)
                for b, sl in enumerate(halves):
                    V.scalar_tensor_tensor(fs[:, j % 2, sl], ps[4][:, sl], cumc[:, b, bass.ds(n, 1)],
                                           fm[:, sl], ALU.add, ALU.add).then_inc(s_S, 1)
                for b, sl in enumerate(halves):
                    dve.wait_ge(s_S, n * 2 + (b + 1))
                    V.tensor_reduce(fst[:, j % 2, b:b + 1], fs[:, j % 2, sl], AX_X, ALU.max,
                                    negate=True).then_inc(s_max, 1)

            def fox_norm(n, j):
                dve.wait_ge(s_exp, n * 2 + 2)
                V.reciprocal(fst[:, j % 2, 4:6], fst[:, j % 2, 2:4]).then_inc(s_ri, 1)

            def fox_out(n, j):
                dve.wait_ge(s_pv, n + 1)
                o = ps[6][:, 0:S]
                V.tensor_scalar(obT[:, bass.ds(n, 1), 0, :], o, 1.0, None, ALU.mult).then_inc(s_ob, 1)
                dve.wait_ge(s_ob, n * 2 + 1)
                V.tensor_tensor(obT[:, bass.ds(n, 1), 1, :], o,
                                obT[:, bass.ds(n, 1), 0, :].bitcast(F32), ALU.subtract).then_inc(s_ob, 1)

            def fox_steps(it):
                st = {}
                for j in range(4):
                    n = it * 4 + j
                    st.setdefault(2 * j, []).append(lambda n=n, j=j: fox_scores(n, j))
                    st.setdefault(2 * j + 1, []).insert(0, lambda n=n, j=j: fox_norm(n, j))
                    st.setdefault(2 * j + 4, []).append(lambda n=n, j=j: fox_out(n, j))
                return st

            def gla_decays(h):
                bh = bT[:, bass.ds(h * 2, 2), :]
                V.tensor_scalar(qd[:], bh, 1.0, None, ALU.mult).then_inc(s_bh, 1)
                dve.wait_ge(s_bh, h * 2 + 1)
                q4 = qd[:].rearrange("p a (c t) -> p (a c) t", t=CH)
                V.tensor_tensor(kd[:].rearrange("p a (c t) -> p (a c) t", t=CH),
                                q4[:, :, CH - 1:CH].broadcast_to([P, 2 * NC, CH]), q4,
                                ALU.subtract).then_inc(s_bh, 1)

            def gla_decayed(h):
                dve.wait_ge(s_e, h * 3 + 3)
                V.tensor_tensor(qd[:], gq[:], ep[:], ALU.mult).then_inc(s_qd, 1)
                V.tensor_tensor(ki[:], gk[:], ki[:], ALU.mult).then_inc(s_qd, 1)
                V.tensor_tensor(kd[:], gk[:], kd[:], ALU.mult).then_inc(s_qd, 1)
                dve.wait_ge(s_qd, h * 5 + 1)
                last = ep[:].rearrange("p a (c t) -> p a c t", t=CH)[:, :, :, CH - 1:CH]
                for a in range(2):
                    i = V.tensor_tensor(qv1[:, a, :, :], qd[:, a, 2 * CH:4 * CH].rearrange("p (c t) -> p c t", t=CH),
                                        last[:, a, 1:3, :].broadcast_to([P, 2, CH]), ALU.mult)
                i.then_inc(s_qd, 1)
                dve.wait_ge(s_qd, h * 5 + 4)
                V.tensor_tensor(qv2[:], qv1[:, :, 1, :], last[:, :, 1, :].broadcast_to([P, 2, CH]),
                                ALU.mult).then_inc(s_qd, 1)

            def gla_mask(h):
                dve.wait_ge(s_at, h * 3 + 3)
                diag = am[:, 0:3:2, :]
                for n, (mask, op) in enumerate(((mhi, ALU.min), (mlo, ALU.max))):
                    V.tensor_tensor(diag, diag, mask[:].unsqueeze(1).broadcast_to([P, 2, P]), op).then_inc(s_am, 1)
                    dve.wait_ge(s_am, h * 2 + (n + 1))

            def gla_out(h):
                newton(s_gy, h + 1, s_gnr, h * 4)
                dve.wait_ge(s_evac, events(GLA, h, 6))
                dve.wait_ge(s_gout, 16)
                for t in range(TT):
                    V.scalar_tensor_tensor(ot[:, t, :], ps[5 + t][:], nst[:, 5, t:t + 1], gout[:],
                                           ALU.mult, ALU.mult).then_inc(s_ot, 1)
                for t in range(TT):
                    dve.wait_ge(s_ot, h * 4 + (t + 1))
                    V.tensor_tensor(ot[:, t, :], ot[:, t, :], gg[:, t, :], ALU.mult).then_inc(s_ot, 1)
                dve.wait_ge(s_ot, h * 4 + 4)

            def gla_split(h, t):
                dve.wait_ge(s_gt, h * 2 + (t + 1))
                o = ps[4 + t][:].rearrange("p (k n) -> p k n", k=4)
                hi = oaT[:, bass.ds(h * 4, 4), 0, t * P:t * P + P]
                V.tensor_scalar(hi, o, 1.0, None, ALU.mult).then_inc(s_oa, 1)
                dve.wait_ge(s_oa, h * 4 + (2 * t + 1))
                V.tensor_tensor(oaT[:, bass.ds(h * 4, 4), 1, t * P:t * P + P], o, hi.bitcast(F32),
                                ALU.subtract).then_inc(s_oa, 1)

            def gla_steps(h):
                return {0: [lambda: gla_decays(h)], 1: [lambda: gla_decayed(h)], 4: [lambda: gla_mask(h)],
                        6: [lambda: norm_mean(h * 2 + 2, s_ss, s_gms, HV)], 7: [lambda: gla_out(h)],
                        9: [lambda: gla_split(h, 0)], 10: [lambda: gla_split(h, 1)]}

            def merge(*ds):
                out_ = {}
                for d_ in ds:
                    for k_, v_ in d_.items():
                        out_.setdefault(k_, []).extend(v_)
                return out_

            def fox_gemm(it):
                return {7: [lambda: join(FOX, it, 0, 0, lambda j: fq[:, j, :], FSC)],
                        15: [lambda: join(FOX, it, 4, 4, lambda j: fk[:, j, :])],
                        22: [lambda: mod_cols(ada_no(FOX, it), it * 4 + 2 * KT)]}

            def gla_gemm(it):
                return {3: [lambda: join(GLA, it, 0, 0, lambda j: gq[:, j, :], GSC, (0, 1))],
                        7: [lambda: join(GLA, it, 2, 2, lambda j: gk[:, j, :], 1.0, (2, 3))],
                        22: [lambda: mod_cols(ada_no(GLA, it), it * 4 + 3 * KT)]}

            def gated(it, e, x_, add):
                before = it * 3 + (1 if add else 0)
                if not (isinstance(before, int) and before == 0):
                    dve.wait_ge(s_m, before)
                for j in range(4):
                    dve.wait_ge(s_tmp, turned(MIX, it, e + j) + 1)
                    V.tensor_tensor(mt[:, j, :], ps[j][:, 0:S], tmp[:, j % 2, :], ALU.add).then_inc(s_evac, 1)
                dve.wait_ge(s_evac, events(MIX, it, e + 3) + 1)
                dve.wait_ge(s_gz, x_ + 1)
                rows = mT[:, bass.ds(it * 4, 4), :]
                if not add:
                    V.tensor_tensor(rows, mt[:], gz[:], ALU.mult).then_inc(s_m, 1)
                else:
                    V.tensor_tensor(mt[:], mt[:], gz[:], ALU.mult).then_inc(s_m, 1)
                    dve.wait_ge(s_m, before + 1)
                    V.tensor_tensor(rows, rows, mt[:], ALU.add).then_inc(s_m, 1)

            def mix_gemm(it):
                return {7: [lambda: join(MIX, it, 0, 0, lambda j: gz[:, j, :])],
                        13: [lambda: mod_row(ada_no(MIX, it), gate1, it * NB)],
                        15: [lambda: gated(it, 4, it * 2, False)],
                        23: [lambda: join(MIX, it, 8, 8, lambda j: gz[:, j, :])],
                        28: [lambda: mod_row(ada_no(MIX, it, 1), gate2, it * NB)],
                        31: [lambda: gated(it, 12, it * 2 + 1, True)]}

            run(FOX, 0, merge(fox_gemm(0), {0: [small_join], 2: [decay_min], 3: [log_sigmoids],
                                            4: [forget_cols], 5: [forget_cums]}))
            with dve.Fori(1, 4) as it:
                run(FOX, it, merge(fox_steps(it - 1), fox_gemm(it)))
            run(GLA, 0, merge(fox_steps(3), gla_gemm(0)))
            with dve.Fori(1, 4) as it:
                run(GLA, it, merge(gla_steps(it - 1), gla_gemm(it)))
            run(MIX, 0, merge(gla_steps(3), mix_gemm(0)))
            with dve.Fori(1, 3) as it:
                run(MIX, it, mix_gemm(it))

            def merged_lo(b):
                dve.wait_ge(s_cvh, b + 1)
                V.tensor_tensor(hT[:, 4 * b:4 * b + 4, 1, :], mT[:, 4 * b:4 * b + 4, :],
                                hT[:, 4 * b:4 * b + 4, 0, :].bitcast(F32), ALU.subtract).then_inc(s_cvl, 1)

            run(MIX, 3, merge(mix_gemm(3), {26: [lambda: merged_lo(0)], 27: [lambda: merged_lo(1)],
                                            29: [lambda: merged_lo(2)]}))
            merged_lo(3)
            V.scalar_tensor_tensor(gcol[:, 1, :], modc[:, 3, :], 1.0, gcol[:, 1, :],
                                   ALU.add, ALU.mult).then_inc(s_acol, 1)

            def residual(ph, it, g, e, b, n, gate, land):
                cols = slice(NB * n, NB * n + NB)
                t5t = t5[:].rearrange("p j n -> p (j n)").rearrange("p (t n) -> p t n", t=TT)
                for t in range(TT):
                    bank_done(dve, ph, it, g, b, t, TT)
                    V.tensor_tensor(t5t[:, t, :], ps[2 * (n % 2) + t][:], gate[:, cols], ALU.mult).then_inc(s_evac, 1)
                if land:
                    dve.wait_ge(s_xl, 16)
                for t in range(TT):
                    dve.wait_ge(s_evac, events(ph, it, e + t) + 1)
                    V.tensor_tensor(xl[:, t, cols], xl[:, t, cols], t5t[:, t, :], ALU.add).then_inc(s_x2, 1)

            run(OUT, 0, {UG * n + UG - 1: [lambda n=n: residual(OUT, 0, UG * n + UG - 1, 2 * n, n, n, gate1, n == 0)]
                         for n in range(4)})
            norm2()

            def ff_up(it, n):
                if n == 0:
                    dve.wait_ge(s_x2, it * 8 + 8)
                else:
                    dve.wait_ge(s_actl, it * 4 + n)
                for j in range(4):
                    dve.wait_ge(s_tmp, turned(FF, it, 4 * n + j) + 1)
                    V.tensor_tensor(t5[:, j, :], ps[j][:, 0:S], tmp[:, j % 2, :], ALU.add).then_inc(s_evac, 1)
                dve.wait_ge(s_evac, events(FF, it, 4 * n + 3) + 1)
                V.scalar_tensor_tensor(t5[:], t5[:], 0.0, t5[:], ALU.max, ALU.mult).then_inc(s_act, 1)

            def ff_lo(it, n):
                dve.wait_ge(s_acth, it * 4 + (n + 1))
                V.tensor_tensor(oaT[:, 4 * n:4 * n + 4, 1, :], t5[:],
                                oaT[:, 4 * n:4 * n + 4, 0, :].bitcast(F32), ALU.subtract).then_inc(s_actl, 1)

            def ff_steps(it):
                st = {UG * n + UG - 1: [lambda n=n: ff_up(it, n)] for n in range(4)}
                for n in range(4):
                    st[UG * n + UG + 1] = [lambda n=n: ff_lo(it, n)]
                    st[UG * (4 + n) + UG - 1] = [lambda n=n: residual(FF, it, UG * (4 + n) + UG - 1, 16 + 2 * n, 12 + n, n, gate2, False)]
                return st

            with dve.Fori(0, 3) as it:
                run(FF, it, ff_steps(it))
            def final_gain(n):
                dve.wait_ge(s_gfin, 16)
                dve.wait_ge(s_nss, 10 + 2 * n + 2)
                cols = slice(n * NB, (n + 1) * NB)
                V.tensor_tensor(xl[:, :, cols], xl[:, :, cols],
                                gfin[:, cols].unsqueeze(1).broadcast_to([P, TT, NB]), ALU.mult).then_inc(s_xg, 1)

            run(FF, 3, merge(ff_steps(3), {UG * (4 + n) + UG + 2: [lambda n=n: final_gain(n)] for n in range(3)}),
                last=FF["n"])
            part_sums(2)
            final_gain(3)
            newton(s_ny, 3, s_nr, 8)
            dve.wait_ge(s_xg, 4)
            for h in range(2):
                half = slice(h * (D // 2), (h + 1) * (D // 2))
                V.tensor_scalar(xl[:, 0, half], xl[:, 0, half], nst[:, 5, 0:1], None, ALU.mult).then_inc(s_yo, 1)

        @block.tensor
        def _(pe):
            T = nc.tensor

            def mod_cols(ag):
                pe.wait_ge(s_ada, ag * (2 * UG) + 2 * UG)
                pe.wait_ge(s_mod, ag)
                for j in range(4):
                    for h in range(2):
                        i = T.matmul(ps[7][:, j:j + 1], acc[:, h, j * P:j * P + P], ones[:, 0:1],
                                     start=(h == 0), stop=(h == 1))
                i.then_inc(s_modmm, 1)

            def mod_row(ag):
                pe.wait_ge(s_ada, ag * (2 * UG) + 2 * UG)
                pe.wait_ge(s_mod, ag)
                for h in range(2):
                    i = T.matmul(ps[7][:], ones[:], acc[:, h, :], start=(h == 0), stop=(h == 1))
                i.then_inc(s_modmm, 1)

            def norm_turn(r, n):
                t, b = n // 4, n % 4
                pe.wait_ge(s_xna if t else s_xnd, r + 1)
                if n >= 4:
                    pe.wait_ge(s_xte, 8 * r + n - 3)
                for k in range(4):
                    i = T.transpose(ps[b][:, k * P:k * P + P],
                                    xn[:, t, (4 * b + k) * P:(4 * b + k + 1) * P], ident[:])
                i.then_inc(s_xt, 1)

            def x2_turn(n):
                for t in range(TT):
                    pe.wait_ge(s_x2, 2 * n + t + 1)
                    pe.wait_ge(s_xte, 8 + (2 * (n - 1) + t + 1 if n else 0))
                    for k in range(4):
                        i = T.transpose(ps[4 + t][:, k * P:k * P + P],
                                        xl[:, t, (4 * n + k) * P:(4 * n + k + 1) * P], ident[:])
                    i.then_inc(s_xt, 1)

            def ada_first(i, par, mm):
                pe.wait_ge((s_raw + s_fraw)[mm], i * 32 + 16 * (par + 1))
                if mm == 0 and not isinstance(i, int):
                    pe.wait_ge(s_row, i * 2 + (par - 1))
                T.matmul(ps[6 + par][0:1, :], cond[:, 2 * mm + 1:2 * mm + 2], first[mm][:, 1, :],
                         start=(mm == 0), stop=False).then_inc(s_adp, 1)

            def sum_first(i, par):
                pe.wait_ge(s_ada, i * (4 * UG) + 2 * UG * (par + 1))
                T.matmul(ps[6 + par][0:1, :], ones[:, 0:1], acc[:, par, :], start=False,
                         stop=True).then_inc(s_rowsum, 1)

            def cols_first(i, par):
                pe.wait_ge(s_row, i * 2 + (par + 1))
                if not isinstance(i, int):
                    pe.wait_ge(s_mod, i * 2 + (par - 1))
                row = tmp[0:1, :, :].rearrange("p a n -> p (a n)")
                for j in range(4):
                    m = T.matmul(ps[4 + par][:, j:j + 1], row[0:1, j * P:j * P + P], ones[0:1, 0:1],
                                 start=True, stop=True)
                m.then_inc(s_modmm, 1)

            def banks_free(ph, it, e, deltas):
                def wait(j):
                    need = events(ph, it, e) + deltas[j]
                    if not (isinstance(need, int) and need <= 0):
                        pe.wait_ge(s_evac, need)
                return wait

            def turned_unit(ph, it, g, e, src, ready, deltas=(-3, -2, -1, 0)):
                g_ = g % UG
                sl = g_slot(ph, g)
                pe.wait_ge(s_lo, g_no(ph, it, g) + 1)
                free = banks_free(ph, it, e, deltas)
                first, final = g_ == 0, g_ == UG - 1
                order = [(j, k) for j in range(4) for k in range(KU)]
                if not first and not final:
                    order = [(j, k) for k in range(KU) for j in range(4)]
                for j, k in order:
                    kt = KU * g_ + k
                    if first and k == 0:
                        free(j)
                    if ready:
                        ready(kt)
                    w = slice(j * P, j * P + P)
                    T.matmul(ps[j][:], whi[sl][:, k, w], src[:, kt, :, :], start=(kt == 0), stop=False,
                             skip_group_check=True)
                    i = T.matmul(ps[j][:, 0:S], wlo[sl][:, k, w], src[:, kt, 0, :], start=False,
                                 stop=(kt == KT - 1), skip_group_check=True)
                    if final and k == KU - 1 and (j, k) != order[-1]:
                        i.then_inc(s_bank, 1)
                i.then_inc(s_pe, 1)

            def head_unit(it, g, e, deltas):
                g_, b0 = g % 4, 2 * (g // 4)
                sl = g_slot(GLA, g)
                pe.wait_ge(s_lo, g_no(GLA, it, g) + 1)
                free = banks_free(GLA, it, e, deltas)
                for j in range(2):
                    if g_ == 0:
                        free(j)
                    for k in range(4):
                        kt = 4 * g_ + k
                        w = slice(j * P, j * P + P)
                        T.matmul(ps[b0 + j][:], by_head(whi[sl])[:, k, w], hT[:, kt, :, :], start=(kt == 0),
                                 stop=False, skip_group_check=True)
                        i = T.matmul(ps[b0 + j][:, 0:S], by_head(wlo[sl])[:, k, w], hT[:, kt, 0, :], start=False,
                                     stop=(kt == KT - 1), skip_group_check=True)
                    if g_ == 3 and j == 0:
                        i.then_inc(s_bank, 1)
                i.then_inc(s_pe, 1)

            def token_unit(ph, it, g, e, src, bank, ready, deltas=(-3, -2)):
                g_ = g % UG
                sl = g_slot(ph, g)
                pe.wait_ge(s_lo, g_no(ph, it, g) + 1)
                free = banks_free(ph, it, e, deltas)
                first, final = g_ == 0, g_ == UG - 1
                order = [(t, k) for t in range(TT) for k in range(KU)]
                for t, k in order:
                    kt = KU * g_ + k
                    if first and k == 0:
                        free(t)
                    if ready:
                        ready(kt)
                    tok = slice(t * P, t * P + P)
                    for n, (hl, w) in enumerate(((0, whi), (0, wlo), (1, whi))):
                        i = T.matmul(ps[bank + t][:], src[:, kt, hl, tok], w[sl][:, k, :],
                                     start=(kt == 0 and n == 0), stop=(kt == KT - 1 and n == 2))
                    if final and k == KU - 1 and (t, k) != order[-1]:
                        i.then_inc(s_bank, 1)
                i.then_inc(s_pe, 1)

            pe.wait_ge(s_vrow, 32)
            pe.wait_ge(s_ident, 1)
            pe.wait_ge(s_ones, 1)
            T.transpose(ps[3][:, 0:2 * KT], vrow[:], ident[0:2 * KT, 0:2 * KT]).then_inc(s_vt, 1)
            pe.wait_ge(s_cond, 1)
            for par in range(2):
                for mm in range(UG):
                    ada_first(0, par, mm)
                    if par == 1 and mm >= 2:
                        if mm == 2:
                            cols_first(0, 0)
                            pe.wait_ge(s_gcol, 1)
                        norm_turn(0, mm - 2)
                sum_first(0, par)
            norm_turn(0, 6)
            norm_turn(0, 7)
            with pe.Fori(1, ADA0 // 2) as i:
                for par in range(2):
                    for mm in range(UG):
                        ada_first(i, par, mm)
                        if mm == 2:
                            cols_first(i if par else i - 1, 1 - par)
                    sum_first(i, par)
            cols_first(ADA0 // 2 - 1, 1)

            pe.wait_ge(s_lo, 1)
            sh, sl_ = small_k(whi[0]), small_k(wlo[0])
            for k in range(KT):
                pe.wait_ge(s_hl, k + 1)
                T.matmul(ps[4][0:CH, :], sh[:, k, :], hT[:, k, :, :], start=(k == 0), stop=False,
                         skip_group_check=True)
                i = T.matmul(ps[4][0:CH, 0:S], sl_[:, k, :], hT[:, k, 0, :], start=False, stop=(k == KT - 1),
                             skip_group_check=True)
            i.then_inc(s_pe, 1)

            def decay_logits():
                pe.wait_ge(s_gl, 1)
                pe.wait_ge(s_wup, 32)
                pe.wait_ge(s_smd, 1)
                pe.wait_ge(s_mod, ADA0)
                for n in range(4):
                    t, a = n // 2, n % 2
                    T.matmul(ps[4 + n][:], gl[:, t * P:t * P + P], wup[:, a, :], start=True,
                             stop=True).then_inc(s_az, 1)

            def forget_turn():
                pe.wait_ge(s_lf, 1)
                pe.wait_ge(s_azd, 4)
                pe.wait_ge(s_aza, 4)
                for t in range(TT):
                    i = T.transpose(ps[7][:, t * FH:t * FH + FH], zm[32:32 + FH, t * P:t * P + P],
                                    ident[32:32 + FH, 32:32 + FH])
                i.then_inc(s_ft, 1)

            def forget_sums():
                pe.wait_ge(s_lft, 1)
                pe.wait_ge(s_mask, 7)
                T.matmul(ps[7][:, 32:48], tri[:], lft[:, 0, :], start=True, stop=True)
                T.matmul(ps[7][:, 48:64], ones[:], lft[:, 0, :], start=True, stop=False)
                T.matmul(ps[7][:, 48:64], tri[:], lft[:, 1, :], start=False, stop=True)
                T.matmul(ps[6][0:FH, 0:P], lft[:, 0, :], tri[:], start=True, stop=True)
                T.matmul(ps[6][0:FH, P:S], lft[:, 0, :], ones[:], start=True, stop=False)
                T.matmul(ps[6][0:FH, P:S], lft[:, 1, :], tri[:], start=False, stop=True).then_inc(s_fc, 1)

            def decay_sums():
                pe.wait_ge(s_la, 1)
                pe.wait_ge(s_fcd, 2)
                lav = la[:].rearrange("p t a n -> p t (a n)")
                for d in range(8):
                    for t in range(TT):
                        o = (d % 2) * S + t * P
                        i = T.matmul(ps[4 + d // 2][:, o:o + P], lav[:, t, d * P:d * P + P], tri16[:],
                                     start=True, stop=True)
                    if d % 2:
                        i.then_inc(s_bt, 1)

            def fox_scores(it, n, j):
                pe.wait_ge(s_evac, events(FOX, it, 8))
                pe.wait_ge(s_rowcum, 16)
                if not (isinstance(n, int) and n == 0):
                    pe.wait_ge(s_S, n * 2)
                for b, (c0, keys) in enumerate(((0, P), (P, S))):
                    T.matmul(ps[4][:, c0:c0 + keys], fq[:, j, b * P:b * P + P], fk[:, j, 0:keys],
                             start=True, stop=False)
                    i = T.matmul(ps[4][:, c0:c0 + keys], ones[0:1, :], ncrow[0:1, bass.ds(n, 1), 0:keys],
                                 start=False, stop=True)
                i.then_inc(s_qk, 1)

            def fox_turn(n, j):
                pe.wait_ge(s_p, n * 2 + 2)
                if not (isinstance(n, int) and n == 0):
                    pe.wait_ge(s_ptc, n)
                for b in range(3):
                    i = T.transpose(ps[5][:, b * P:b * P + P], fs[:, j % 2, b * P:b * P + P], ident[:])
                i.then_inc(s_pt, 1)

            def fox_pv(n, j):
                pe.wait_ge(s_ptc, n + 1)
                if not (isinstance(n, int) and n == 0):
                    pe.wait_ge(s_ob, n * 2)
                v = slice(j * FD, j * FD + FD)
                T.matmul(ps[6][:, 0:P], fv[:, 0, v], pT[:, 0:P], start=True, stop=True)
                T.matmul(ps[6][:, P:S], fv[:, 0, v], pT[:, P:2 * P], start=True, stop=False)
                T.matmul(ps[6][:, P:S], fv[:, 1, v], pT[:, 2 * P:3 * P], start=False, stop=True).then_inc(s_pv, 1)

            def fox_steps(it):
                st = {}
                for j in range(4):
                    n = it * 4 + j
                    st.setdefault(2 * j + 4, []).append(lambda n=n, j=j: fox_pv(n, j))
                for j in range(4):
                    n = it * 4 + j
                    st.setdefault(2 * j + 3, []).append(lambda n=n, j=j: fox_turn(n, j))
                for j in range(4):
                    n = it * 4 + j
                    st.setdefault(2 * j, []).append(lambda n=n, j=j: fox_scores(it, n, j))
                return st

            def gla_scores(h):
                pe.wait_ge(s_qd, h * 5 + 5)
                if not (isinstance(h, int) and h == 0):
                    pe.wait_ge(s_oa, h * 4)
                ch = lambda t_, a, cc: t_[:, a, cc * CH:cc * CH + CH]
                jobs = []
                for cc in range(NC):
                    r0 = (cc % 2) * CH
                    c0 = cc * CH if cc < 2 else 3 * P - 4 * CH + cc * CH
                    jobs.append((r0, c0, ki, cc, lambda a, cc=cc: ch(qd, a, cc)))
                    for q_ in range(cc + 1, NC):
                        c0 = q_ * CH if cc < 2 else 3 * P - 4 * CH + q_ * CH
                        far = q_ - cc
                        if far == 1:
                            rhs = lambda a, q_=q_: ch(qd, a, q_)
                        elif far == 2:
                            rhs = lambda a, q_=q_: qv1[:, a, q_ - 2, :]
                        else:
                            rhs = lambda a: qv2[:, a, :]
                        jobs.append((r0, c0, kd, cc, rhs))
                for r0, c0, keys, cc, rhs in jobs:
                    for a in range(2):
                        i = T.matmul(ps[4][r0:r0 + CH, c0:c0 + CH], ch(keys, a, cc), rhs(a),
                                     start=(a == 0), stop=(a == 1))
                i.then_inc(s_ga, 1)

            def gla_values(h):
                pe.wait_ge(s_am, h * 2 + 2)
                T.matmul(ps[5][:], am[:, 0, :], gv[:, 0, :], start=True, stop=True)
                T.matmul(ps[6][:], am[:, 1, :], gv[:, 0, :], start=True, stop=False)
                T.matmul(ps[6][:], am[:, 2, :], gv[:, 1, :], start=False, stop=True).then_inc(s_go, 1)

            def gla_turn(h):
                for t in range(TT):
                    pe.wait_ge(s_ot, h * 4 + (TT + t + 1))
                    for k in range(4):
                        i = T.transpose(ps[4 + t][:, k * P:k * P + P], ot[:, t, k * P:k * P + P], ident[:])
                    i.then_inc(s_gt, 1)

            def gla_steps(h):
                return {3: [lambda: gla_scores(h)], 5: [lambda: gla_values(h)], 9: [lambda: gla_turn(h)]}

            def merge(*ds):
                out_ = {}
                for d_ in ds:
                    for k_, v_ in d_.items():
                        out_.setdefault(k_, []).extend(v_)
                return out_

            def run(ph, it, steps, unit):
                for g in range(ph["n"]):
                    for step in steps.get(g, ()):
                        step()
                    unit(g)

            def fox(it, steps):
                def unit(g):
                    n = g // UG
                    if n < 2:
                        turned_unit(FOX, it, g, 4 * n, hT, None, (-3, -2, -1, 0) if n else (-1, 0, 0, 0))
                    else:
                        token_unit(FOX, it, g, 8, hT, 0, None, (-3, 0))
                run(FOX, it, merge(steps, {21: [lambda: mod_cols(ada_no(FOX, it))]}), unit)

            def gla(it, steps):
                def unit(g):
                    n = g // UG
                    if n == 0:
                        head_unit(it, g, 0, (-3, -2) if g < 4 and not isinstance(it, int) else (-1, 0))
                    elif n == 1:
                        token_unit(GLA, it, g, 4, hT, 0, None, (-2, 0))
                    else:
                        token_unit(GLA, it, g, 6, hT, 2, None, (-2, -2))
                run(GLA, it, merge(steps, {21: [lambda: mod_cols(ada_no(GLA, it))]}), unit)

            def mix(it, steps):
                def unit(g):
                    n = g // UG
                    if g == UG:
                        pe.wait_ge(s_ob, 2 * FH)
                    if g == 3 * UG:
                        pe.wait_ge(s_oa, 4 * 4)
                    turned_unit(MIX, it, g, 4 * n, (hT, obT, hT, oaT)[n], None)
                run(MIX, it, merge(steps, {13: [lambda: mod_row(ada_no(MIX, it))],
                                           27: [lambda: mod_row(ada_no(MIX, it, 1))]}), unit)

            fox(0, {2: [decay_logits], 4: [forget_turn], 5: [forget_sums], 6: [decay_sums]})
            with pe.Fori(1, 4) as it:
                fox(it, fox_steps(it - 1))
            gla(0, fox_steps(3))
            with pe.Fori(1, 4) as it:
                gla(it, gla_steps(it - 1))
            mix(0, gla_steps(3))
            with pe.Fori(1, 4) as it:
                mix(it, {})
            run(OUT, 0, {UG * n + UG + 2: [lambda n=n: x2_turn(n)] for n in range(3)}, lambda g: token_unit(
                OUT, 0, g, 2 * (g // UG), hT, 2 * (g // UG % 2),
                (lambda kt: pe.wait_ge(s_cvl, kt // 4 + 1)) if g < UG else None))
            x2_turn(3)
            pe.wait_ge(s_rd, 2)
            for t in range(TT):
                i = T.matmul(ps[6][:, t * P:t * P + P], ones[:], rdiag[:, t, :], start=True, stop=True)
            i.then_inc(s_rrow, 1)

            def ff(it):
                def unit(g):
                    n = g // UG
                    if n < 4:
                        ready = None
                        if n == 0:
                            ready = (lambda kt: pe.wait_ge(s_hl, KT + kt + 1))
                        turned_unit(FF, it, g, 4 * n, obT, ready)
                    else:
                        ready = None
                        if n == 4:
                            ready = (lambda kt: pe.wait_ge(s_actl, it * 4 + (kt // 4 + 1)))
                        token_unit(FF, it, g, 8 + 2 * n, oaT, 2 * (n % 2), ready)
                run(FF, it, {}, unit)

            with pe.Fori(0, 4) as it:
                ff(it)


NAMES = ["x", "c", "w_ada", "b_ada", "g_norm1", "w_in", "w_gla_a_up", "b_gla_a", "g_gla_out", "b_fox_f",
         "w_proj_gla", "w_proj_fox", "w_out", "g_norm2", "w_ff1", "w_ff2", "g_final"]


def kernel(**inputs):
    import numpy as np
    import concourse.bacc as bacc
    from concourse.bass_utils import run_bass_kernel_spmd

    nc = bacc.Bacc("TRN2", target_bir_lowering=False, num_devices=1)
    arrays, args = {}, []
    for name in NAMES:
        a = np.ascontiguousarray(inputs[name])
        arrays[f"in_{name}"] = a
        args.append(nc.dram_tensor(f"in_{name}", a.shape, mybir.dt.from_np(a.dtype), kind="ExternalInput").ap())
    args.append(nc.dram_tensor("out_0", (1, S, D), F32, kind="ExternalOutput").ap())
    build(nc, *args)
    r = run_bass_kernel_spmd(nc, [arrays], core_ids=[0])
    return r.results[0]["out_0"]
```
